# Optimizing a Trainium2 kernel written in Bass

```python
import math
import jax
import jax.numpy as jnp
from jax import lax
import numpy as np

D_MODEL = 2048
BATCH = 1
SEQ = 256
DEPTH = 2

CHUNK = 64
N_A_LAYERS = DEPTH // 2
N_B_LAYERS = DEPTH - N_A_LAYERS
MEM_LEN = 256
MEM_HEADS = 4
MEM_WIDTH = D_MODEL // 4
MEM_HEAD_DIM = MEM_WIDTH // MEM_HEADS
MAIN_WIDTH = D_MODEL - MEM_WIDTH
SSM_HEAD_DIM = 64
SSM_HEADS = MAIN_WIDTH // SSM_HEAD_DIM
SSM_GROUPS = 4
SSM_STATE = 128
CONV_WIDTH = 4
SSM_CONV_DIM = MAIN_WIDTH + 2 * SSM_GROUPS * SSM_STATE
IN_A_WIDTH = MAIN_WIDTH + SSM_CONV_DIM + SSM_HEADS + MEM_WIDTH
DT_MIN = 1e-3
DT_MAX = 1e-1
ATTN_HEAD_DIM = 64
ATTN_HEADS = MAIN_WIDTH // ATTN_HEAD_DIM
KV_HEADS = 4
WINDOW = 128
WINDOW_CHUNKS = WINDOW // CHUNK
ROPE_THETA = 10000.0
IN_B_WIDTH = MAIN_WIDTH + MEM_WIDTH
KV_WIDTH = 2 * KV_HEADS * ATTN_HEAD_DIM
PEER_HEADS = 8
PEER_KEYS = 128
PEER_EXPERTS = PEER_KEYS * PEER_KEYS
PEER_QUERY_DIM = 128
PEER_TOPK = 16
PEER_BLOCK = 128
DEEPNORM_ALPHA = (2.0 * DEPTH) ** 0.25
DEEPNORM_BETA = (8.0 * DEPTH) ** -0.25
LN_EPS = 1e-5
RMS_EPS = 1e-5

kernel_name = 'hybrid_ssd_swa_peer_yoco_block'

def layer_norm(x, g, b):
    xf = x.astype(jnp.float32)
    mu = jnp.mean(xf, axis=-1, keepdims=True)
    var = jnp.mean(jnp.square(xf - mu), axis=-1, keepdims=True)
    return ((xf - mu) * lax.rsqrt(var + LN_EPS) * g.astype(jnp.float32) + b.astype(jnp.float32)).astype(x.dtype)

def grouped_rms_norm(y, g):
    b, s, w = y.shape
    yg = y.reshape(b, s, SSM_GROUPS, w // SSM_GROUPS)
    yg = yg * lax.rsqrt(jnp.mean(jnp.square(yg), axis=-1, keepdims=True) + RMS_EPS)
    return yg.reshape(b, s, w) * g.astype(jnp.float32)

def rope_tables(positions, dim):
    inv = 1.0 / (ROPE_THETA ** (jnp.arange(0, dim, 2, dtype=jnp.float32) / dim))
    ang = positions.astype(jnp.float32)[..., None] * inv
    return jnp.cos(ang), jnp.sin(ang)

def apply_rope(t, cos, sin):
    t1, t2 = jnp.split(t, 2, axis=-1)
    c = cos[:, :, None, :].astype(t.dtype)
    s = sin[:, :, None, :].astype(t.dtype)
    return jnp.concatenate([t1 * c - t2 * s, t1 * s + t2 * c], axis=-1)

def causal_depthwise_conv(u, w, bias):
    ch = u.shape[-1]
    out = lax.conv_general_dilated(u, w[:, None, :].astype(u.dtype), window_strides=(1,),
                                   padding=[(CONV_WIDTH - 1, 0)],
                                   dimension_numbers=('NWC', 'WIO', 'NWC'),
                                   feature_group_count=ch)
    return out + bias.astype(u.dtype)

def ssd_chunked(xs, dt, a, bm, cm):
    b, s, h, p = xs.shape
    nc = s // CHUNK
    r = h // SSM_GROUPS
    f32 = jnp.float32
    xdt = (xs.astype(f32) * dt[..., None]).reshape(b, nc, CHUNK, SSM_GROUPS, r, p)
    a_dt = (dt * a).reshape(b, nc, CHUNK, SSM_GROUPS, r)
    a_cs = jnp.cumsum(a_dt, axis=2)
    bc = bm.astype(f32).reshape(b, nc, CHUNK, SSM_GROUPS, SSM_STATE)
    cc = cm.astype(f32).reshape(b, nc, CHUNK, SSM_GROUPS, SSM_STATE)
    seg = a_cs[:, :, :, None] - a_cs[:, :, None, :]
    tri = jnp.tril(jnp.ones((CHUNK, CHUNK), dtype=bool))[None, None, :, :, None, None]
    l_dec = jnp.exp(jnp.where(tri, seg, -jnp.inf))
    cb = jnp.einsum('bclgn,bcsgn->bclsg', cc, bc)
    y_diag = jnp.einsum('bclsg,bclsgr,bcsgrp->bclgrp', cb, l_dec, xdt)
    decay_states = jnp.exp(a_cs[:, :, -1:] - a_cs)
    states = jnp.einsum('bclgn,bclgr,bclgrp->bcgrpn', bc, decay_states, xdt)
    chunk_decay = jnp.exp(a_cs[:, :, -1])

    def step(hst, inp):
        st, dec = inp
        return dec[..., None, None] * hst + st, hst

    init = jnp.zeros((b, SSM_GROUPS, r, p, SSM_STATE), f32)
    _, prev = lax.scan(step, init, (jnp.swapaxes(states, 0, 1), jnp.swapaxes(chunk_decay, 0, 1)))
    prev = jnp.swapaxes(prev, 0, 1)
    y_off = jnp.einsum('bclgn,bcgrpn,bclgr->bclgrp', cc, prev, jnp.exp(a_cs))
    return (y_diag + y_off).reshape(b, s, h, p)

def mamba2_mixer(z, xbc, dt_raw, conv_w, conv_b, dt_bias, a_log, d_skip, norm_g):
    b, s, _ = z.shape
    f32 = jnp.float32
    xbc = jax.nn.silu(causal_depthwise_conv(xbc, conv_w, conv_b))
    xs = xbc[..., :MAIN_WIDTH].reshape(b, s, SSM_HEADS, SSM_HEAD_DIM)
    bm = xbc[..., MAIN_WIDTH:MAIN_WIDTH + SSM_GROUPS * SSM_STATE].reshape(b, s, SSM_GROUPS, SSM_STATE)
    cm = xbc[..., MAIN_WIDTH + SSM_GROUPS * SSM_STATE:].reshape(b, s, SSM_GROUPS, SSM_STATE)
    dt = jax.nn.softplus(dt_raw.astype(f32) + dt_bias.astype(f32))
    a = -jnp.exp(a_log.astype(f32))
    y = ssd_chunked(xs, dt, a, bm, cm)
    y = y + xs.astype(f32) * d_skip.astype(f32)[:, None]
    y = y.reshape(b, s, MAIN_WIDTH) * jax.nn.silu(z.astype(f32))
    return grouped_rms_norm(y, norm_g).astype(z.dtype)

def chunk_band(t):
    b, s, kh, d = t.shape
    nc = s // CHUNK
    tc = t.reshape(b, nc, CHUNK, kh, d)
    tp = jnp.pad(tc, ((0, 0), (WINDOW_CHUNKS - 1, 0), (0, 0), (0, 0), (0, 0)))
    return jnp.concatenate([tp[:, i:i + nc] for i in range(WINDOW_CHUNKS)], axis=2)

def sliding_window_attention(q, k_band, v_band, band_valid, sinks):
    b, s, h, d = q.shape
    nc = s // CHUNK
    grp = h // KV_HEADS
    qc = q.reshape(b, nc, CHUNK, KV_HEADS, grp, d)
    sc = jnp.einsum('bclkgd,bcwkd->bckglw', qc, k_band).astype(jnp.float32) * (d ** -0.5)
    sc = jnp.where(band_valid[None, :, None, None, None, :], sc, -jnp.inf)
    sink = jnp.broadcast_to(sinks.astype(jnp.float32).reshape(1, 1, KV_HEADS, grp, 1, 1),
                            (b, nc, KV_HEADS, grp, CHUNK, 1))
    probs = jax.nn.softmax(jnp.concatenate([sc, sink], axis=-1), axis=-1)[..., :-1]
    out = jnp.einsum('bckglw,bcwkd->bclkgd', probs.astype(v_band.dtype), v_band)
    return out.reshape(b, s, h * d)

def memory_attention(mq, mem, w_mem_kv):
    b, s, _ = mq.shape
    m = mem.shape[1]
    q = mq.reshape(b, s, MEM_HEADS, MEM_HEAD_DIM)
    kv = mem @ w_mem_kv
    k = kv[..., :MEM_WIDTH].reshape(b, m, MEM_HEADS, MEM_HEAD_DIM)
    v = kv[..., MEM_WIDTH:].reshape(b, m, MEM_HEADS, MEM_HEAD_DIM)
    sc = jnp.einsum('bshd,bmhd->bhsm', q, k).astype(jnp.float32) * (MEM_HEAD_DIM ** -0.5)
    probs = jax.nn.softmax(sc, axis=-1)
    return jnp.einsum('bhsm,bmhd->bshd', probs.astype(v.dtype), v).reshape(b, s, MEM_WIDTH)

def peer_ffn(x, wq, subkeys, u, v):
    b, s, dm = x.shape
    q = (x @ wq).reshape(b, s, PEER_HEADS, 2, PEER_QUERY_DIM // 2)
    sc = jnp.einsum('bshtd,htkd->bshtk', q, subkeys).astype(jnp.float32)
    top_s, top_i = lax.top_k(sc, PEER_TOPK)
    cand = top_s[..., 0, :, None] + top_s[..., 1, None, :]
    cand = cand.reshape(b, s, PEER_HEADS, PEER_TOPK * PEER_TOPK)
    best_s, best_c = lax.top_k(cand, PEER_TOPK)
    i1 = jnp.take_along_axis(top_i[..., 0, :], best_c // PEER_TOPK, axis=-1)
    i2 = jnp.take_along_axis(top_i[..., 1, :], best_c % PEER_TOPK, axis=-1)
    idx = i1 * PEER_KEYS + i2
    gate = jax.nn.softmax(best_s, axis=-1).astype(x.dtype)
    n_tok = b * s
    nsel = PEER_HEADS * PEER_TOPK
    xt = x.reshape(n_tok // PEER_BLOCK, PEER_BLOCK, dm)
    it = idx.reshape(n_tok // PEER_BLOCK, PEER_BLOCK, nsel)
    gt = gate.reshape(n_tok // PEER_BLOCK, PEER_BLOCK, nsel)

    def block(args):
        xb, ib, gb = args
        hid = jnp.einsum('td,tkd->tk', xb, u[ib])
        act = jax.nn.gelu(hid, approximate=False) * gb
        return jnp.einsum('tk,tkd->td', act, v[ib])

    out = lax.map(block, (xt, it, gt))
    return out.reshape(b, s, dm)

def setup_inputs(seed: int = 0) -> dict:
    key = jax.random.key(seed)
    ks = jax.random.split(key, 24)
    f32 = jnp.float32
    nrm = lambda k, shp, sc: jax.random.normal(k, shp, f32) * sc
    x = nrm(ks[0], (BATCH, SEQ, D_MODEL), 1.0)
    mem = nrm(ks[1], (BATCH, MEM_LEN, D_MODEL), 1.0)
    positions = jnp.broadcast_to(jnp.arange(SEQ, dtype=jnp.int32)[None, :], (BATCH, SEQ))
    w_in_a = nrm(ks[2], (N_A_LAYERS, D_MODEL, IN_A_WIDTH), D_MODEL ** -0.5)
    conv_w = nrm(ks[3], (N_A_LAYERS, CONV_WIDTH, SSM_CONV_DIM), CONV_WIDTH ** -0.5)
    conv_b = nrm(ks[4], (N_A_LAYERS, SSM_CONV_DIM), 0.01)
    uu = jax.random.uniform(ks[5], (N_A_LAYERS, SSM_HEADS), f32)
    dt0 = jnp.exp(uu * (math.log(DT_MAX) - math.log(DT_MIN)) + math.log(DT_MIN))
    dt_bias = dt0 + jnp.log(-jnp.expm1(-dt0))
    a_log = jnp.log(jax.random.uniform(ks[6], (N_A_LAYERS, SSM_HEADS), f32, minval=1.0, maxval=16.0))
    d_skip = 1.0 + nrm(ks[7], (N_A_LAYERS, SSM_HEADS), 0.1)
    ssm_norm_g = 1.0 + nrm(ks[8], (N_A_LAYERS, MAIN_WIDTH), 0.02)
    w_kv_shared = nrm(ks[9], (D_MODEL, KV_WIDTH), D_MODEL ** -0.5)
    w_in_b = nrm(ks[10], (N_B_LAYERS, D_MODEL, IN_B_WIDTH), D_MODEL ** -0.5)
    attn_sinks = nrm(ks[11], (N_B_LAYERS, ATTN_HEADS), 0.5)
    w_mem_kv = nrm(ks[12], (DEPTH, D_MODEL, 2 * MEM_WIDTH), D_MODEL ** -0.5)
    w_out = nrm(ks[13], (DEPTH, D_MODEL, D_MODEL), DEEPNORM_BETA * D_MODEL ** -0.5)
    ln_g = 1.0 + nrm(ks[14], (DEPTH, 2, D_MODEL), 0.02)
    ln_b = nrm(ks[15], (DEPTH, 2, D_MODEL), 0.02)
    peer_wq = nrm(ks[16], (DEPTH, D_MODEL, PEER_HEADS * PEER_QUERY_DIM), D_MODEL ** -0.5)
    peer_subkeys = nrm(ks[17], (DEPTH, PEER_HEADS, 2, PEER_KEYS, PEER_QUERY_DIM // 2), (PEER_QUERY_DIM // 2) ** -0.5)
    peer_u = nrm(ks[18], (DEPTH, PEER_EXPERTS, D_MODEL), D_MODEL ** -0.5)
    peer_v = nrm(ks[19], (DEPTH, PEER_EXPERTS, D_MODEL), DEEPNORM_BETA)
    return {'x': x, 'mem': mem, 'positions': positions, 'w_in_a': w_in_a, 'conv_w': conv_w,
            'conv_b': conv_b, 'dt_bias': dt_bias, 'a_log': a_log, 'd_skip': d_skip,
            'ssm_norm_g': ssm_norm_g, 'w_kv_shared': w_kv_shared, 'w_in_b': w_in_b,
            'attn_sinks': attn_sinks, 'w_mem_kv': w_mem_kv, 'w_out': w_out, 'ln_g': ln_g,
            'ln_b': ln_b, 'peer_wq': peer_wq, 'peer_subkeys': peer_subkeys, 'peer_u': peer_u,
            'peer_v': peer_v}

def reference(x, mem, positions, w_in_a, conv_w, conv_b, dt_bias, a_log, d_skip, ssm_norm_g,
              w_kv_shared, w_in_b, attn_sinks, w_mem_kv, w_out, ln_g, ln_b, peer_wq,
              peer_subkeys, peer_u, peer_v):
    b, s, _ = x.shape
    nc = s // CHUNK
    cos, sin = rope_tables(positions, ATTN_HEAD_DIM)
    slot_chunk = jnp.arange(WINDOW) // CHUNK - (WINDOW_CHUNKS - 1)
    band_valid = (jnp.arange(nc)[:, None] + slot_chunk[None, :]) >= 0
    k_band = None
    v_band = None
    o_z = MAIN_WIDTH
    o_c = o_z + SSM_CONV_DIM
    o_d = o_c + SSM_HEADS
    for l in range(DEPTH):
        if l < N_A_LAYERS:
            i = l
            proj = x @ w_in_a[i]
            main = mamba2_mixer(proj[..., :o_z], proj[..., o_z:o_c], proj[..., o_c:o_d],
                                conv_w[i], conv_b[i], dt_bias[i], a_log[i], d_skip[i], ssm_norm_g[i])
            mq = proj[..., o_d:]
        else:
            j = l - N_A_LAYERS
            if j == 0:
                kv = x @ w_kv_shared
                k = apply_rope(kv[..., :KV_WIDTH // 2].reshape(b, s, KV_HEADS, ATTN_HEAD_DIM), cos, sin)
                v = kv[..., KV_WIDTH // 2:].reshape(b, s, KV_HEADS, ATTN_HEAD_DIM)
                k_band = chunk_band(k)
                v_band = chunk_band(v)
            proj = x @ w_in_b[j]
            q = apply_rope(proj[..., :MAIN_WIDTH].reshape(b, s, ATTN_HEADS, ATTN_HEAD_DIM), cos, sin)
            main = sliding_window_attention(q, k_band, v_band, band_valid, attn_sinks[j])
            mq = proj[..., MAIN_WIDTH:]
        mem_out = memory_attention(mq, mem, w_mem_kv[l])
        mixed = jnp.concatenate([main, mem_out], axis=-1) @ w_out[l]
        x = layer_norm(DEEPNORM_ALPHA * x + mixed, ln_g[l, 0], ln_b[l, 0])
        ffn = peer_ffn(x, peer_wq[l], peer_subkeys[l], peer_u[l], peer_v[l])
        x = layer_norm(DEEPNORM_ALPHA * x + ffn, ln_g[l, 1], ln_b[l, 1])
    return x


_drawn_inputs = setup_inputs


def setup_inputs(seed=0):
    import zlib

    import numpy as np

    out = dict(_drawn_inputs(seed))
    spreads = {}
    factors = {'attn_sinks': 8.0}
    for name, (base, spread) in spreads.items():
        noise = np.random.default_rng([zlib.crc32(name.encode()), seed]).standard_normal(out[name].shape)
        drawn = base * np.exp(spread * noise) if base else spread * noise
        out[name] = jnp.asarray(drawn.astype(out[name].dtype))
    for name, factor in factors.items():
        out[name] = (out[name] * factor).astype(out[name].dtype)
    return out
```

```python
import concourse.bass as bass
from concourse import mybir

F32 = mybir.dt.float32
F32R = mybir.dt.float32r
U32 = mybir.dt.uint32
I32 = mybir.dt.int32
BF16 = mybir.dt.bfloat16
ALU = mybir.AluOpType
ACT = mybir.ActivationFunctionType
AX = mybir.AxisListType

P = 128
TOK = 256
NT = TOK // P
D = 2048
KC = D // P
PC = D // 2
RING = 4
QX = 4
CQ = KC // QX
AHEAD = 3
MEM_HEADS, MEM_D = 4, 128
MAIN = 1536
MC = MAIN // P
GROUPS = 4
GC = MC // GROUPS
SSM_HEADS = 24
CONV_W = 4
XBC_C = 20
ATT_HEADS = 24
KV_HEADS = 4
PEER_H = 8
KEYS = 128
TOPK = 16
UNITS = NT * PEER_H
PITCH = TOK + 4
LPAD = CONV_W - 1
ALPHA = 4.0 ** 0.25
LN_EPS = 1e-5
RMS_EPS = 1e-5
NEG = -3.0e38
MASKED = -1.0e30

S_MEM, S_INA, S_OUT, S_WQ, S_EXP, S_INB = 16, 36, KC, PEER_H, KEYS, 20
P_MEM = 0
P_INA = P_MEM + 2 * S_MEM
P_OUT0 = P_INA + 2 * S_INA
P_WQ0 = P_OUT0 + 2 * S_OUT
P_U0 = P_WQ0 + 2 * S_WQ
P_V0 = P_U0 + 2 * S_EXP
P_INB = P_V0 + 2 * S_EXP
P_OUT1 = P_INB + 2 * S_INB
P_WQ1 = P_OUT1 + 2 * S_OUT
P_U1 = P_WQ1 + 2 * S_WQ
P_V1 = P_U1 + 2 * S_EXP
P_END = P_V1 + 2 * S_EXP
T_MEM = 0
T_INA = T_MEM + S_MEM
T_WQ0 = T_INA + S_INA
T_U0 = T_WQ0 + S_WQ
T_INB = T_U0 + S_EXP
T_WQ1 = T_INB + S_INB
T_U1 = T_WQ1 + S_WQ

C_CONVW, C_CONVB = 0, XBC_C * CONV_W
C_DSKIP = C_CONVB + XBC_C
C_NORMG = C_DSKIP + MC
C_LN = C_NORMG + MC
C_FREQ = C_LN + 4 * 2 * KC
C_COLS = C_FREQ + 1
R_DTB, R_ALOG, R_SINK = C_COLS, C_COLS + 24, C_COLS + 48
R_EPS = C_COLS + 72
PAR = R_EPS + 1

K_IDENT, K_IOTA, K_TRI, K_STRICT = 0, 128, 256, 384
K_ROT, K_DUP, K_MASK = 512, 640, 896
K_COLS = K_MASK + 512

BODY = 4
TRIPS = UNITS
assert 2 * TRIPS * BODY == S_EXP and TRIPS * 16 == TOK


class Chain:

    def __init__(self, eng, sem, settled=None):
        self.settled = settled
        self.eng, self.sem, self.n, self.loop = eng, sem, 0, None

    def value(self):
        if self.loop is None:
            return self.n
        i, start, per, base = self.loop
        return (i - start) * per + (base + self.n)

    def mark(self, ins):
        ins.then_inc(self.sem, 1)
        self.n += 1

    def sync(self):
        self.eng.wait_ge(self.sem, self.value())

    def settle(self):
        self.sync()
        self.eng.sem_inc(self.settled, 1)

    def settle_link(self, ins):
        self.mark(ins)
        self.settle()

    def link(self, ins):
        self.mark(ins)
        self.sync()

    def enter(self, i, start, per):
        self.loop = (i, start, per, self.n)
        self.n = 0

    def leave(self, trips):
        _, _, per, base = self.loop
        assert self.n == per, self.n
        self.loop, self.n = None, base + per * trips


def build(nc, dram):
    ctxs = []

    def sem(name):
        c = nc.semaphore(name)
        ctxs.append(c)
        return c.__enter__()

    at = [(nc.sbuf_base + 31) // 32 * 32]

    def sb(name, shape, dt, offset=None):
        size = 4
        for n in shape[1:]:
            size *= n
        if offset is None:
            offset = at[0]
            at[0] += (size + 31) // 32 * 32
        return nc.alloc_sbuf_tensor_at(name, shape, dt, offset=offset)

    arena_at = at[0]
    arena = sb("arena", [P, S_EXP * TOK], F32)
    xh = sb("xh", [P, KC, TOK], F32R)
    xl = sb("xl", [P, KC, TOK], F32R)
    raw = sb("raw", [P, RING, PC], F32)
    wh = sb("wh", [P, RING, PC], F32R)
    wl = sb("wl", [P, RING, PC], F32R)
    hring = sb("hring", [P, BODY, TOK], F32)
    act_at = at[0]
    act_t = sb("act_t", [P, 2, TOK], F32)
    act_h = sb("act_h", [P, 2, TOK], F32R)
    act_l = sb("act_l", [P, 2, TOK], F32R)
    hot = sb("hot", [P, 2, 4, P], F32, offset=act_at)
    sel_at = at[0]
    sel_t = sb("sel_t", [P, 3, TOK], F32)
    base_c = sb("base_c", [P, 2, P], F32)
    par = sb("par", [P, PAR], F32)
    assert at[0] <= nc.sbuf_usable_end, at[0]
    ident, iota = base_c[:, 0, :], base_c[:, 1, :]
    epsc = par[:, R_EPS:R_EPS + 1]

    def A(off, *shape, dt=F32):
        n = 1
        for k in shape:
            n *= k
        assert off + n <= S_EXP * TOK
        v = arena[:, off:off + n]
        if dt is not F32:
            v = v.bitcast(dt)
        names = "abcd"[:len(shape)]
        if len(shape) == 1:
            return v
        return v.rearrange(f"p ({' '.join(names)}) -> p {' '.join(names)}",
                           **{c: k for c, k in zip(names[1:], shape[1:])})

    psc = nc.psum_tensor("ps", [P, 8, 512], F32)
    ctxs.append(psc)
    ps = psc.__enter__()

    proj = A(0, S_INA, PITCH)
    xc = A(9360, XBC_C, TOK)
    cat = A(14480, KC, TOK)
    kvt = A(18576, 8, TOK)
    vn = A(20624, 2, 512)
    in_raw = A(24464, KC, TOK)
    xdt = A(21648, NT, SSM_HEADS, 64)
    cbm = A(24720, GROUPS, 384)
    ex = A(27024, 2, 384)
    mt = A(27792, 2, 384)
    lcon = A(28560, 3, P)
    dtw = A(28944, KC, SSM_HEADS)
    dts = A(29328, 12, 48)
    nrm = A(29904, 4, TOK)
    ysq = A(0, 2, GC, TOK)
    tri_r = nc.alloc_sbuf_tensor_at("tri_r", [P, 2, P], F32R, offset=arena_at + 4 * 31000)
    adt_r = nc.alloc_sbuf_tensor_at("adt_r", [P, 2, 48], F32R, offset=arena_at + 4 * 31256)
    ident_b, later_b = A(31360, P // 2, dt=BF16), A(31424, P // 2, dt=BF16)
    ssb = A(0, 3, 4, TOK)
    pt = A(3072, 2, 2, 2, TOK)
    asm = A(5120, 3, 5, 4)
    proj1 = A(9360, S_INB, TOK)
    kdup = A(21648, KV_HEADS, TOK)
    vn1 = A(22672, NT, TOK)
    rcon = A(23184, 7, P)
    cs = A(24080, 2, TOK)
    rtmp = A(24592, 2, 2, TOK)
    posi = A(25616, TOK, dt=I32)
    ang = A(25872, 6, TOK)
    kvt_all = A(0, S_MEM, TOK)
    vn_spill = A(4096, 2, 512)
    xn = A(0, NT, D)
    xt = A(4096, KC, TOK)
    lnst = A(20200, NT, 4, 6)
    lnmv = A(20300, NT, 8)
    sc = A(0, UNITS, 2, KEYS)
    qt = A(8192, PEER_H, TOK)
    subk = A(10240, PEER_H, KEYS)
    sw = A(11264, 2, 2, KEYS)
    top_v = A(11776, 2, TOPK)
    top_i = A(11808, 2, TOPK, dt=U32)
    top_f = A(11840, 2, TOPK)
    cand = A(11872, 2, TOPK, TOPK)
    best_v = A(12384, TOPK)
    best_i = A(12400, 3, TOPK, dt=U32)
    best_f = A(12448, 2, TOPK)
    pick = A(12480, 2 * TOPK, TOPK)
    sel = A(12992, 3, UNITS * TOPK)
    gsm = A(13760, 2, UNITS)
    gate_of = A(0, KEYS, TOK)
    al_c = nc.alloc_sbuf_tensor_at("al_c", [P, 2, P], F32R, offset=sel_at)
    alf = nc.alloc_sbuf_tensor_at("alf", [P, P], F32, offset=sel_at + 8 * P)[:, :]

    raw_full = [sem(f"raw_full{j}") for j in range(RING)]
    hi_ready, lo_ready, piece_used = sem("hi_ready"), sem("lo_ready"), sem("piece_used")
    evac_done = sem("evac_done")
    consts_in, l0_in, subk_in, l1_in = (sem(n) for n in ("consts_in", "l0_in", "subk_in", "l1_in"))
    memx_in = [sem(f"memx_in{q}") for q in range(QX)]
    eps_set = sem("eps_set")
    xh_ready, x_ready = sem("xh_ready"), sem("x_ready")
    vtr_ready, vn_ready, spill_done = sem("vtr_ready"), sem("vn_ready"), sem("spill_done")
    conv_done, silu_done = sem("conv_done"), sem("silu_done")
    dt_ready, dtx_ready, dte_ready, dtl_in, dtl_ready = (
        sem(n) for n in ("dt_ready", "dtx_ready", "dte_ready", "dtl_in", "dtl_ready"))
    adt_ready, cs_ready, cs_evac = sem("adt_ready"), sem("cs_ready"), sem("cs_evac")
    cb_ready, cbm_ready = sem("cb_ready"), sem("cbm_ready")
    cbo_ready = sem("cbo_ready")
    xst_ready, xdt_ready = sem("xst_ready"), sem("xdt_ready")
    row_ready, ex_ready, m_ready = (sem(n) for n in ("row_ready", "ex_ready", "m_ready"))
    adth_ready, adtr_ready = sem("adth_ready"), sem("adtr_ready")
    y_ready, y_done = sem("y_ready"), sem("y_done")
    ysq_ready, ms_ready, rms_ready, cat_ready = (sem(n) for n in ("ysq_ready", "ms_ready", "rms_ready", "cat_ready"))
    s_ready, negm_ready, p_ready, pn_ready = (sem(n) for n in ("s_ready", "negm_ready", "p_ready", "pn_ready"))
    pt_ready, pt_evac, o_ready, o_evac = (sem(n) for n in ("pt_ready", "pt_evac", "o_ready", "o_evac"))
    acth_ready, actl_ready, act_ready = sem("acth_ready"), sem("actl_ready"), sem("act_ready")
    al_h_ready, al_ready = sem("al_h_ready"), sem("al_ready")
    alf_ready = sem("alf_ready")
    var_ready, std_ready, rstd_ready = sem("var_ready"), sem("std_ready"), sem("rstd_ready")
    xn_ready, xtr_ready, xta_ready = sem("xn_ready"), sem("xtr_ready"), sem("xta_ready")
    xtd_ready = sem("xtd_ready")
    sc_ready, sc_evac = sem("sc_ready"), sem("sc_evac")
    gd_ready, ge_ready, sel_ready, selt_ready, selt_evac = (
        sem(n) for n in ("gd_ready", "ge_ready", "sel_ready", "selt_ready", "selt_evac"))
    hot_ready, g_ready, g_evac = sem("hot_ready"), sem("g_ready"), sem("g_evac")
    h_stored = [sem(f"h_stored{j}") for j in range(BODY)]
    h_loaded = [sem(f"h_loaded{j}") for j in range(BODY)]
    trig_in, trig_ready, cossin_ready = sem("trig_in"), sem("trig_ready"), sem("cossin_ready")
    rot_ready, rope_done, kdup_ready, kdup_evac = (sem(n) for n in ("rot_ready", "rope_done", "kdup_ready", "kdup_evac"))
    vtr1_ready, vn1_ready = sem("vtr1_ready"), sem("vn1_ready")
    out_done = sem("out_done")
    act_own, dve_own, dve_settled = sem("act_own"), sem("dve_own"), sem("dve_settled")

    w_in, u_in, v_in = dram["w"], dram["u"], dram["v"]
    h_dram, spill = dram["h"], dram["spill"]

    ATT = [[(0, m) for m in range(2)], [(1, c) for c in range(MC)] + [(0, m) for m in range(2)]]
    ATT0 = [0, 2]
    block_cm = nc.Block()
    block = block_cm.__enter__()

    @block.sync
    def _(sp):
        def piece(src, row, p, j, first=False):
            if not first:
                sp.wait_ge(lo_ready, p - (RING - 1))
            sp.dma_start(raw[:, j, :], src[row, :, :]).then_inc(raw_full[j], 16)

        def stream(src, row0, p0, n):
            with sp.Fori(0, n // RING) as i:
                for j in range(RING):
                    piece(src, i * RING + (row0 + j), i * RING + (p0 + j), j)

        def load_x(name, q):
            sp.dma_start(in_raw[:, q * CQ:(q + 1) * CQ, :], dram[name][:, q * CQ:(q + 1) * CQ, :])\
                .then_inc(memx_in[q], 16)

        for q in range(QX):
            load_x("memT", q)
            piece(w_in, q, q, q, first=True)
        for dst, name in ((base_c[:, :, :], "base"), (par[:, 0:C_COLS], "cols")):
            sp.dma_start(dst, dram[name]).then_inc(consts_in, 16)
        sp.dma_start(par[:, C_COLS:R_EPS], dram["rows"].partition_broadcast(P)).then_inc(consts_in, 16)
        sp.dma_start(lcon[:, 0:2, :], dram["tri"]).then_inc(l0_in, 16)
        sp.dma_start(dtw[:, :, :], dram["dtw"]).then_inc(l0_in, 16)
        stream(w_in, RING, RING, 2 * S_MEM - RING)
        for q in range(QX):
            sp.wait_ge(x_ready, q + 1)
            load_x("xT", q)
        sp.wait_ge(vn_ready, 4)
        sp.dma_start(spill[:, 0:1024], kvt_all[:, 8:12, :]).then_inc(spill_done, 16)
        sp.dma_start(spill[:, 1024:2048], vn_spill[:, :, :]).then_inc(spill_done, 16)
        stream(w_in, P_INA, P_INA, 2 * (S_INA + S_OUT + S_WQ))

        def experts(layer, u0, v0):
            row0 = layer * 2 * S_EXP
            sp.wait_ge(x_ready, QX * (3 if layer == 0 else 5))
            sp.dma_start(subk[:, :, :], dram["subk"][layer, :, :, :]).then_inc(subk_in, 16)

            def u_trip(i):
                for j in range(2 * BODY):
                    piece(u_in, i * (2 * BODY) + (row0 + j), i * (2 * BODY) + (u0 + j), j % RING)

            def store(i):
                for j in range(BODY):
                    sp.wait_ge(evac_done, i * BODY + ((T_U0, T_U1)[layer] + j + 1))
                    sp.dma_start(h_dram[i * BODY + j, :, :], hring[:, j, :]).then_inc(h_stored[j], 16)

            u_trip(0)
            with sp.Fori(1, S_EXP // BODY) as i:
                u_trip(i)
                store(i - 1)
            store(S_EXP // BODY - 1)
            for n in range(RING):
                piece(v_in, row0 + n, v0 + n, n)
            for j in range(BODY):
                sp.wait_ge(h_stored[j], 16 * (layer + 1) * (S_EXP // BODY))
                sp.dma_start(hring[:, j, :], h_dram[j, :, :]).then_inc(h_loaded[j], 16)
            for n in range(RING, 2 * BODY):
                piece(v_in, row0 + n, v0 + n, n % RING)

            def v_trip(i):
                for j in range(BODY):
                    sp.wait_ge(act_ready, i * BODY + (layer * S_EXP + j - BODY + 1))
                    sp.dma_start(hring[:, j, :], h_dram[i * BODY + j, :, :]).then_inc(h_loaded[j], 16)
                    for n in (2 * j, 2 * j + 1):
                        piece(v_in, i * (2 * BODY) + (row0 + n), i * (2 * BODY) + (v0 + n), n % RING)

            with sp.Fori(1, S_EXP // BODY) as i:
                v_trip(i)

        experts(0, P_U0, P_V0)
        for j in range(RING):
            piece(w_in, P_INB - 4 * S_EXP + j, P_INB + j, j)
        sp.wait_ge(x_ready, QX * 4)
        sp.dma_start(rcon[:, :, :], dram["rcon"]).then_inc(l1_in, 16)
        sp.dma_start(posi, dram["pos"].partition_broadcast(P)).then_inc(l1_in, 16)
        sp.wait_ge(spill_done, 32)
        sp.dma_start(kvt[:, 0:4, :], spill[:, 0:1024]).then_inc(l1_in, 16)
        sp.dma_start(vn[:, :, :], spill[:, 1024:2048]).then_inc(l1_in, 16)
        stream(w_in, P_INB - 4 * S_EXP + RING, P_INB + RING, 2 * (S_INB + S_OUT + S_WQ) - RING)
        experts(1, P_U1, P_V1)
        sp.wait_ge(xta_ready, 4 * 8)
        sp.wait_ge(xtd_ready, 4 * 8)
        sp.dma_start(dram["out"], xt[:, :, :]).then_inc(out_done, 16)
        sp.wait_ge(out_done, 16)

    @block.scalar
    def _(act):
        own = Chain(act, act_own)

        def hi(p, j, first=False):
            if first:
                act.wait_ge(raw_full[j], 16)
            else:
                act.wait_ge(piece_used, p - (RING - 1))
                act.wait_ge(raw_full[j], raw_count(p, j))
            nc.scalar.activation(wh[:, j, :], raw[:, j, :], ACT.Copy).then_inc(hi_ready, 1)

        def raw_count(p, j):
            return (p - j) * (16 // RING) + 16

        def ahead(p0):
            for n in range(AHEAD):
                hi(p0 + n, n)

        def t_stage(p0, t0, n, evac, lead_first=False, done=0):
            def two(i, first):
                for s in range(2):
                    for e in range(2):
                        j = 2 * s + e
                        if not first or j >= done:
                            hi(i * RING + (p0 + j), j, first=lead_first and first)
                    if not (first and s == 0):
                        k = i * 2 + (s - 1)
                        act.wait_ge(piece_used, k * 2 + (p0 + 2))
                        evac(k, (s + 1) % 2)

            two(0, True)
            if n > 2:
                with act.Fori(1, n // 2) as i:
                    two(i, False)
            act.wait_ge(piece_used, p0 + 2 * n)
            evac(n - 1, 1)

        def copy_out(dst):
            def evac(k, bank):
                nc.scalar.activation(dst(k), ps[:, bank, 0:TOK], ACT.Copy).then_inc(evac_done, 1)
            return evac

        def n_stage(p0, s0, n, source, ready):
            with act.Fori(0, n // 2) as i:
                for s in range(2):
                    for e in range(2):
                        hi(i * RING + (p0 + 2 * s + e), 2 * s + e)
                    ready(i, s)
                    nc.scalar.activation(act_h[:, s, :], source(i, s), ACT.Copy).then_inc(acth_ready, 1)

        def split_input(n):
            for q in range(QX):
                act.wait_ge(memx_in[q], 16 * (n + 1))
                nc.scalar.activation(xh[:, q * CQ:(q + 1) * CQ, :], in_raw[:, q * CQ:(q + 1) * CQ, :],
                                     ACT.Copy).then_inc(xh_ready, 1)

        def attention(layer):
            n0 = ATT0[layer]

            def exps(g, swa):
                s = (n0 + g) % 3
                act.wait_ge(negm_ready, n0 + g + 1)
                for u in range(4):
                    last = nc.scalar.activation(ssb[:, s, u, :], ssb[:, s, u, :], ACT.Exp,
                                                bias=asm[:, s, 1, u:u + 1], accum_out=asm[:, s, 2, u:u + 1])
                    if u < 3 or swa:
                        own.mark(last)
                    else:
                        last.then_inc(p_ready, 1)
                if swa:
                    nc.scalar.activation(asm[:, s, 3, :], asm[:, s, 4, :], ACT.Exp).then_inc(p_ready, 1)

            groups = ATT[layer]
            for i in range(len(groups) + 3):
                if i < len(groups):
                    exps(i, groups[i][0])
                if 0 <= i - 2 < len(groups):
                    g = n0 + i - 2
                    act.wait_ge(pt_ready, g + 1)
                    if i - 2 >= 2:
                        act.wait_ge(o_ready, g - 1)
                    nc.scalar.activation(pt[:, g % 2, :, :, :], ps[:, 4:6, :].rearrange("p a (b c) -> p a b c", b=2),
                                         ACT.Copy).then_inc(pt_evac, 1)
                if 0 <= i - 3 < len(groups):
                    g = n0 + i - 3
                    swa, c = groups[i - 3]
                    act.wait_ge(o_ready, g + 1)
                    if swa:
                        nc.scalar.activation(cat[:, c, :], ps[:, 6 + g % 2, 0:TOK], ACT.Copy).then_inc(o_evac, 1)
                    else:
                        nc.scalar.activation(cat[:, MC + 2 * c:MC + 2 * c + 2, :],
                                             ps[:, 6 + g % 2, :].rearrange("p (a b) -> p a b", a=2),
                                             ACT.Copy).then_inc(o_evac, 1)

        def alpha(n):
            act.wait_ge(alf_ready, n + 1)
            nc.scalar.activation(al_c[:, 0, :], alf, ACT.Copy).then_inc(al_h_ready, 1)

        def norm(n, p_next):
            if n < 3:
                ahead(p_next)
            act.wait_ge(var_ready, n + 1)
            nc.scalar.activation(lnmv[:, :, 2:3], lnmv[:, :, 1:2], ACT.Sqrt, bias=epsc).then_inc(std_ready, 1)
            act.wait_ge(rstd_ready, n + 1)
            nc.scalar.activation(xn[:, 0, :], ps[:, 0:4, :].rearrange("p a b -> p (a b)"), ACT.Identity,
                                 bias=lnmv[:, 0, 4:5], scale=lnmv[:, 0, 3:4]).then_inc(xn_ready, 1)
            for q in range(QX):
                b = 2 * q
                act.wait_ge(xtr_ready, 8 * n + b + 1)
                for c in (2 * b, 2 * b + 1):
                    gain, shift = C_LN + 2 * n * KC + c, C_LN + (2 * n + 1) * KC + c
                    nc.scalar.activation(xt[:, c, :], ps[:, b, (c % 2) * TOK:(c % 2 + 1) * TOK], ACT.Identity,
                                         bias=par[:, shift:shift + 1], scale=par[:, gain:gain + 1])\
                        .then_inc(xta_ready, 1)
                if n < 3:
                    act.wait_ge(xta_ready, 8 * n + 2 * (q + 1))
                    act.wait_ge(xtd_ready, 8 * n + 2 * (q + 1))
                    nc.scalar.activation(xh[:, q * CQ:(q + 1) * CQ, :], xt[:, q * CQ:(q + 1) * CQ, :],
                                         ACT.Copy).then_inc(xh_ready, 1)

        def experts(layer, u0, v0, t0):
            def gelu(k, slot, bank):
                act.wait_ge(piece_used, k * 2 + (u0 + 2))
                stores = (k - slot) * (16 // BODY) + layer * 16 * (S_EXP // BODY)
                if not (isinstance(k, int) and stores == 0):
                    act.wait_ge(h_stored[slot], stores)
                nc.scalar.activation(hring[:, slot, :], ps[:, bank, 0:TOK], ACT.Gelu).then_inc(evac_done, 1)

            def gates_out(q, k):
                act.wait_ge(g_ready, q + (layer * TOK // 4 + 1))
                nc.scalar.activation(gate_of[:, :, bass.ds(q * 4, 4)].rearrange("p i t -> p t i"),
                                     ps[:, 2 + k % 2, :].rearrange("p (t i) -> p t i", t=4),
                                     ACT.Copy).then_inc(g_evac, 1)

            def trip(i, first, spread, spread_first=False):
                for s in range(BODY):
                    for e in range(2):
                        hi(i * (2 * BODY) + (u0 + 2 * s + e), (2 * s + e) % RING)
                    if not (first and s == 0):
                        gelu(i * BODY + (s - 1), (s - 1) % BODY, (s + 1) % 2)
                    if spread and not (spread_first and s == 0):
                        gates_out((i - TRIPS) * 4 + (s - 1), (s - 1) % 4)

            trip(0, True, False)
            trip(1, False, False)
            with act.Fori(2, TRIPS) as i:
                trip(i, False, False)
            act.wait_ge(gd_ready, layer + 1)
            nc.scalar.activation(sel[:, 2, :], sel[:, 2, :], ACT.Exp).then_inc(ge_ready, 1)
            for w in range(3):
                act.wait_ge(selt_ready, layer * 3 + w + 1)
                nc.scalar.activation(sel_t[:, w, :], ps[:, 2 + w, 0:TOK], ACT.Copy).then_inc(selt_evac, 1)
            trip(TRIPS, False, True, True)
            with act.Fori(TRIPS + 1, 2 * TRIPS) as i:
                trip(i, False, True)
            gelu(S_EXP - 1, BODY - 1, 1)
            gates_out(TOK // 4 - 1, 3)

            alpha(2 * layer + 1)

            def ready(i, s):
                act.wait_ge(act_ready, i * 2 + (layer * S_EXP + s + 1))
            n_stage(v0, layer * S_EXP, S_EXP, lambda i, s: act_t[:, s, :], ready)

        split_input(0)
        t_stage(P_MEM, T_MEM, S_MEM, copy_out(lambda k: kvt_all[:, k, :]), lead_first=True)
        for n in range(4):
            act.wait_ge(vtr_ready, n + 1)
            dst = vn[:, n, :] if n < 2 else vn_spill[:, n - 2, :]
            nc.scalar.activation(dst, ps[:, 2 + n, :], ACT.Copy).then_inc(vn_ready, 1)
        nc.scalar.activation(kvt[:, 0:4, :], kvt_all[:, 0:4, :], ACT.Copy).then_inc(vn_ready, 1)
        act.wait_ge(piece_used, P_MEM + 2 * S_MEM)
        split_input(1)
        act.wait_ge(spill_done, 32)
        act.wait_ge(vn_ready, 5)
        t_stage(P_INA, T_INA, S_INA, copy_out(lambda k: proj[:, k, LPAD:LPAD + TOK]))

        act.wait_ge(dtx_ready, 1)
        own.mark(nc.scalar.activation(dts[:, 2, :], dts[:, 1, :], ACT.Exp, scale=-1.0))
        nc.scalar.activation(dts[:, 4, 0:24], par[:, R_ALOG:R_ALOG + 24], ACT.Exp).then_inc(dte_ready, 1)
        own.sync()
        nc.scalar.activation(dts[:, 3, :], dts[:, 2, :], ACT.Ln, bias=1.0).then_inc(dtl_ready, 1)
        act.wait_ge(conv_done, 1)
        nc.scalar.activation(xc[:, MC:XBC_C, :], xc[:, MC:XBC_C, :], ACT.Silu).then_inc(silu_done, 1)
        nc.scalar.activation(xc[:, 0:MC, :], xc[:, 0:MC, :], ACT.Silu).then_inc(silu_done, 1)
        act.wait_ge(evac_done, T_INA + S_INA)
        nc.scalar.activation(proj[:, XBC_C:XBC_C + MC, LPAD:LPAD + TOK],
                             proj[:, XBC_C:XBC_C + MC, LPAD:LPAD + TOK], ACT.Silu).then_inc(silu_done, 1)
        act.wait_ge(adt_ready, 1)
        nc.scalar.activation(adt_r[:, 0, :], dts[:, 6, :], ACT.Copy).then_inc(adth_ready, 1)
        for g in range(GROUPS):
            act.wait_ge(cb_ready, g + 1)
            nc.scalar.activation(cbm[:, g, P:2 * P], ps[:, 2 + g, P:2 * P], ACT.Copy).then_inc(cbo_ready, 1)
        act.wait_ge(cs_evac, 1)
        for h in range(SSM_HEADS):
            s = h % 2
            act.wait_ge(row_ready, h + 1)
            if h >= 2:
                act.wait_ge(m_ready, h - 1)
            bias = (dts[:, 7, h:h + 1], dts[:, 8, h:h + 1], dts[:, 7, 24 + h:25 + h])
            for b in range(3):
                ins = nc.scalar.activation(ex[:, s, b * P:(b + 1) * P], ps[:, 6 + s, b * P:(b + 1) * P], ACT.Exp,
                                           bias=bias[b])
                if b < 2:
                    own.mark(ins)
                else:
                    ins.then_inc(ex_ready, 1)
        for g in range(GROUPS):
            act.wait_ge(y_done, MC)
            if g >= 2:
                act.wait_ge(ms_ready, g - 1)
            nc.scalar.activation(ysq[:, g % 2, :, :], cat[:, g * GC:(g + 1) * GC, :], ACT.Square).then_inc(ysq_ready, 1)
            act.wait_ge(ms_ready, g + 1)
            if g == 0:
                act.wait_ge(eps_set, 1)
            nc.scalar.activation(nrm[:, g, :], ps[:, 2 + g % 2, 0:TOK], ACT.Sqrt, bias=epsc).then_inc(rms_ready, 1)
        attention(0)
        alpha(0)
        act.wait_ge(cat_ready, 1)
        act.wait_ge(o_evac, 2)
        n_stage(P_OUT0, 0, S_OUT, lambda i, s: cat[:, i * 2 + s, :], lambda i, s: None)
        norm(0, P_WQ0)
        t_stage(P_WQ0, T_WQ0, S_WQ, copy_out(lambda k: qt[:, k, :]), done=AHEAD)
        experts(0, P_U0, P_V0, T_U0)
        norm(1, P_INB)

        t_stage(P_INB, T_INB, S_INB, copy_out(lambda k: proj1[:, k, :]), done=AHEAD)
        act.wait_ge(trig_in, 1)
        nc.scalar.activation(cs[:, :, :], ang[:, 0:2, :], ACT.Sin).then_inc(cossin_ready, 1)
        for k in range(KV_HEADS):
            act.wait_ge(kdup_ready, k + 1)
            nc.scalar.activation(kdup[:, k, :], ps[:, 2 + k, 0:TOK], ACT.Copy).then_inc(kdup_evac, 1)
        act.wait_ge(vtr1_ready, 1)
        nc.scalar.activation(vn1[:, :, :], ps[:, 6, :].rearrange("p (a b) -> p a b", a=2), ACT.Copy).then_inc(vn1_ready, 1)
        attention(1)
        alpha(2)
        act.wait_ge(o_evac, 16)
        n_stage(P_OUT1, 0, S_OUT, lambda i, s: cat[:, i * 2 + s, :], lambda i, s: None)
        norm(2, P_WQ1)
        t_stage(P_WQ1, T_WQ1, S_WQ, copy_out(lambda k: qt[:, k, :]), done=AHEAD)
        experts(1, P_U1, P_V1, T_U1)
        norm(3, None)

    @block.tensor
    def _(pe):
        def mm(out, lhs, rhs, start, stop, **kw):
            return nc.tensor.matmul(out, lhs, rhs, start=start, stop=stop, **kw)

        def slab_t(piece, slab, par_, s4, first=False, x_from=None):
            if not first:
                pe.wait_ge(evac_done, slab - 1)
            out = ps[:, par_, 0:TOK]
            for e in range(2):
                j = (2 * s4 + e) % RING
                pe.wait_ge(lo_ready, piece + (e + 1))
                for k in range(KC // 2):
                    kc = e * (KC // 2) + k
                    if x_from is not None and kc % CQ == 0:
                        pe.wait_ge(x_ready, x_from + kc // CQ + 1)
                    w_hi, w_lo = (w[:, j, k * P:(k + 1) * P] for w in (wh, wl))
                    mm(out, w_hi, xh[:, kc, :], kc == 0, False)
                    mm(out, w_hi, xl[:, kc, :], False, False)
                    last = mm(out, w_lo, xh[:, kc, :], False, kc == KC - 1)
                last.then_inc(piece_used, 1)

        def t_stage(p0, t0, n, x_count):
            lead = t0 == 0
            for s in range(2):
                slab_t(p0 + 2 * s, t0 + s, s, s, first=lead, x_from=QX * (x_count - 1) if s == 0 else None)
            with pe.Fori(1, n // 2) as i:
                for s in range(2):
                    slab_t(i * RING + (p0 + 2 * s), i * 2 + (t0 + s), s, s)

        def slab_n(piece, chunk, s):
            pe.wait_ge(actl_ready, chunk + 1)
            for e in range(2):
                j = 2 * s + e
                pe.wait_ge(lo_ready, piece + (e + 1))
                for t in range(NT):
                    a_h, a_l = (a[:, s, t * P:(t + 1) * P] for a in (act_h, act_l))
                    for q in range(2):
                        out = ps[:, 4 * t + 2 * e + q, :]
                        w_hi, w_lo = (w[:, j, q * 512:(q + 1) * 512] for w in (wh, wl))
                        mm(out, a_h, w_hi, False, False, skip_group_check=True)
                        mm(out, a_h, w_lo, False, False, skip_group_check=True)
                    for q in range(2):
                        last = mm(ps[:, 4 * t + 2 * e + q, :], a_l, wh[:, j, q * 512:(q + 1) * 512], False, False,
                                  skip_group_check=True)
                last.then_inc(piece_used, 1)

        def n_stage(k, p0, c0, n):
            pe.wait_ge(al_ready, k + 1)
            for t in range(NT):
                for c in range(KC):
                    out = ps[:, 4 * t + c // 4, (c % 4) * P:(c % 4 + 1) * P]
                    x_h, x_l = (x[:, c, t * P:(t + 1) * P] for x in (xh, xl))
                    mm(out, x_h, al_c[:, 0, :], c % 4 == 0, False, skip_group_check=True)
                    mm(out, x_h, al_c[:, 1, :], False, False, skip_group_check=True)
                    mm(out, x_l, al_c[:, 0, :], False, False, skip_group_check=True)
            with pe.Fori(0, n // 2) as i:
                for s in range(2):
                    slab_n(i * RING + (p0 + 2 * s), i * 2 + (c0 + s), s)

        def to_dims(n):
            pe.wait_ge(xn_ready, 2 * n + 2)
            for b in range(8):
                for c in range(2):
                    for t in range(NT):
                        last = nc.tensor.transpose(ps[:, b, c * TOK + t * P:c * TOK + (t + 1) * P],
                                                   xn[:, t, (2 * b + c) * P:(2 * b + c + 1) * P], ident)
                last.then_inc(xtr_ready, 1)

        def attention(layer):
            n0, groups = ATT0[layer], ATT[layer]

            def scores(g):
                swa, c = groups[g]
                s = (n0 + g) % 2
                if g >= 2:
                    pe.wait_ge(negm_ready, n0 + g - 1)
                for r in range(2):
                    for t in range(NT):
                        out = ps[:, 2 * s + r, t * TOK:(t + 1) * TOK]
                        if swa:
                            rows = slice(64 * r, 64 * r + 64)
                            last = mm(out, proj1[rows, 4 + c, t * P:(t + 1) * P],
                                      kdup[rows, 2 * c // (ATT_HEADS // KV_HEADS), :], True, True)
                        else:
                            h = 2 * c + r
                            q = proj1[:, 16 + h, :] if layer else proj[:, XBC_C + MC + h, LPAD:LPAD + TOK]
                            last = mm(out, q[:, t * P:(t + 1) * P], kvt[:, h, :], True, True)
                last.then_inc(s_ready, 1)

            for i in range(len(groups) + 3):
                if i < len(groups):
                    scores(i)
                if 0 <= i - 2 < len(groups):
                    g = n0 + i - 2
                    pe.wait_ge(pn_ready, g + 1)
                    if i - 2 >= 1:
                        pe.wait_ge(pt_evac, g)
                    for r in range(2):
                        for t in range(NT):
                            for k in range(2):
                                last = nc.tensor.transpose(ps[:, 4 + r, k * TOK + t * P:k * TOK + (t + 1) * P],
                                                           ssb[:, g % 3, 2 * r + t, k * P:(k + 1) * P], ident)
                    last.then_inc(pt_ready, 1)
                if 0 <= i - 3 < len(groups):
                    g = n0 + i - 3
                    swa, c = groups[i - 3]
                    pe.wait_ge(pt_evac, g + 1)
                    if i - 3 >= 2:
                        pe.wait_ge(o_evac, g - 1)
                    for r in range(2):
                        for k in range(2):
                            if swa:
                                kv = 2 * c // (ATT_HEADS // KV_HEADS)
                                last = mm(ps[64 * r:64 * r + 64, 6 + g % 2, 0:TOK], vn1[:, k, kv * 64:kv * 64 + 64],
                                          pt[:, g % 2, r, k, :], k == 0, k == 1)
                            else:
                                h = 2 * c + r
                                last = mm(ps[:, 6 + g % 2, r * TOK:(r + 1) * TOK], vn[:, k, h * P:(h + 1) * P],
                                          pt[:, g % 2, r, k, :], k == 0, k == 1)
                    last.then_inc(o_ready, 1)

        def experts(layer, u0, v0, t0):
            pe.wait_ge(subk_in, 16 * (layer + 1))
            pe.wait_ge(evac_done, t0)
            for b in range(UNITS // 4):
                if b == 3:
                    pe.wait_ge(sc_evac, 4 * layer + 1)
                for u4 in range(4):
                    u = 4 * b + u4
                    t, h = u // PEER_H, u % PEER_H
                    for half in range(2):
                        rows = slice(64 * half, 64 * half + 64)
                        last = mm(ps[:, 2 + 2 * (b % 3) + half, u4 * P:(u4 + 1) * P],
                                  qt[rows, h, t * P:(t + 1) * P], subk[rows, h, :], True, True)
                last.then_inc(sc_ready, 1)

            def trip(i, spread):
                for s in range(BODY):
                    piece = i * (2 * BODY) + (u0 + 2 * s)
                    slab_t(piece, i * BODY + (t0 + s), s % 2, s)
                    if spread:
                        q = (i - TRIPS) * 4 + s
                        pe.wait_ge(hot_ready, q + (layer * TOK // 4 + 1))
                        if not isinstance(q, int) or layer or q >= 2:
                            pe.wait_ge(g_evac, q + (layer * TOK // 4 - 1))
                        for t in range(4):
                            last = mm(ps[:, 2 + s % 2, t * P:(t + 1) * P], hot[:, 0, t, :], hot[:, 1, t, :],
                                      True, True)
                        last.then_inc(g_ready, 1)

            with pe.Fori(0, TRIPS) as i:
                trip(i, False)
            for w in range(3):
                pe.wait_ge(sel_ready, layer + 1)
                for t in range(NT):
                    last = nc.tensor.transpose(ps[:, 2 + w, t * P:(t + 1) * P], sel[:, w, t * P:(t + 1) * P], ident)
                last.then_inc(selt_ready, 1)
            trip(TRIPS, True)
            with pe.Fori(TRIPS + 1, 2 * TRIPS) as i:
                trip(i, True)
            pe.wait_ge(evac_done, t0 + S_EXP)
            pe.wait_ge(g_evac, (layer + 1) * TOK // 4)
            n_stage(2 * layer + 1, v0, (layer + 1) * S_OUT + layer * S_EXP, S_EXP)

        pe.wait_ge(consts_in, 48)
        t_stage(P_MEM, T_MEM, S_MEM, 1)
        pe.wait_ge(evac_done, T_MEM + S_MEM)
        for n in range(4):
            for h in range(MEM_HEADS):
                last = nc.tensor.transpose(ps[:, 2 + n, h * P:(h + 1) * P],
                                           kvt_all[:, 8 * (n // 2) + 4 + h, (n % 2) * P:(n % 2 + 1) * P], ident)
            last.then_inc(vtr_ready, 1)
        pe.wait_ge(l0_in, 32)
        pe.wait_ge(vn_ready, 5)
        pe.wait_ge(x_ready, 2 * QX)
        for t in range(NT):
            for c in range(KC):
                for x in (xh, xl):
                    last = mm(ps[:, 7, t * 24:(t + 1) * 24], x[:, c, t * P:(t + 1) * P].bitcast(F32), dtw[:, c, :],
                              c == 0 and x is xh, c == KC - 1 and x is xl)
        last.then_inc(dt_ready, 1)
        t_stage(P_INA, T_INA, S_INA, 2)

        tri, strict = lcon[:, 0, :], lcon[:, 1, :]
        pe.wait_ge(adt_ready, 1)
        mm(ps[:, 6, 0:48], tri, dts[:, 6, :], True, True)
        mm(ps[:, 6, 64:88], strict, dts[:, 6, 0:24], True, True).then_inc(cs_ready, 1)
        pe.wait_ge(silu_done, 1)
        for g in range(GROUPS):
            b_t, c_t = xc[:, MC + g, :], xc[:, MC + GROUPS + g, :]
            mm(ps[:, 2 + g, 0:TOK], b_t[:, 0:P], c_t, True, True)
            mm(ps[:, 2 + g, TOK:TOK + P], b_t[:, P:TOK], c_t[:, P:TOK], True, True).then_inc(cb_ready, 1)
        pe.wait_ge(silu_done, 2)
        pe.wait_ge(evac_done, T_INA + S_INA)
        for b in range(6):
            if b >= 2:
                pe.wait_ge(cbm_ready, b - 1)
                pe.wait_ge(cbo_ready, b - 1)
            for c in range(2):
                for t in range(NT):
                    last = nc.tensor.transpose(ps[:, b, c * TOK + t * P:c * TOK + (t + 1) * P],
                                               xc[:, 2 * b + c, t * P:(t + 1) * P], ident)
            last.then_inc(xst_ready, 1)
        pe.wait_ge(cs_evac, 1)
        pe.wait_ge(xdt_ready, 6)

        pe.wait_ge(adtr_ready, 1)

        def rows(h):
            if h >= 2:
                pe.wait_ge(ex_ready, h - 1)
            bank = ps[:, 6 + h % 2, :]
            for k in range(2):
                a0, a1 = (adt_r[:, k, t * 24 + h:t * 24 + h + 1].broadcast_to([P, P]) for t in range(NT))
                mm(bank[:, 0:P], a0, tri_r[:, 0, :], k == 0, False, skip_group_check=True)
                mm(bank[:, P:3 * P], a1, tri_r[:, :, :], False, False, skip_group_check=True)
            mm(bank[:, 0:P], ident_b, later_b, False, False, skip_group_check=True)
            mm(bank[:, 2 * P:3 * P], ident_b, later_b, False, True, skip_group_check=True).then_inc(row_ready, 1)

        rows(0)
        for h in range(SSM_HEADS):
            if h + 1 < SSM_HEADS:
                rows(h + 1)
            c, r, s = h // 2, h % 2, h % 2
            pe.wait_ge(m_ready, h + 1)
            if c >= 2 and r == 0:
                pe.wait_ge(y_done, c - 1)
            mm(ps[64 * r:64 * r + 64, c % 2, 0:TOK], xdt[:, 0, h, :], mt[:, s, 0:TOK], True, False)
            mm(ps[64 * r:64 * r + 64, c % 2, P:TOK], xdt[:, 1, h, :], mt[:, s, TOK:TOK + P], False, True)\
                .then_inc(y_ready, 1)
        for g in range(GROUPS):
            pe.wait_ge(ysq_ready, g + 1)
            if g >= 2:
                pe.wait_ge(rms_ready, g - 1)
            for c in range(GC):
                last = mm(ps[:, 2 + g % 2, 0:TOK], lcon[:, 2, :], ysq[:, g % 2, c, :], c == 0, c == GC - 1)
            last.then_inc(ms_ready, 1)
        pe.wait_ge(y_done, MC)
        pe.wait_ge(rms_ready, GROUPS)
        attention(0)
        pe.wait_ge(o_evac, 2)
        n_stage(0, P_OUT0, 0, S_OUT)
        to_dims(0)
        t_stage(P_WQ0, T_WQ0, S_WQ, 3)
        experts(0, P_U0, P_V0, T_U0)
        to_dims(1)

        t_stage(P_INB, T_INB, S_INB, 4)
        pe.wait_ge(l1_in, 64)
        pe.wait_ge(evac_done, T_INB + S_INB)
        for n in range(14):
            c = n if n < 2 else n + 2
            if n >= 2:
                pe.wait_ge(rope_done, n - 1)
            mm(ps[:, n % 2, 0:TOK], rcon[:, 0, :], proj1[:, c, :], True, True).then_inc(rot_ready, 1)
        for k in range(KV_HEADS):
            pe.wait_ge(rope_done, 2)
            mm(ps[:, 2 + k, 0:TOK], rcon[:, 1 + k % 2, :], proj1[:, k // 2, :], True, True).then_inc(kdup_ready, 1)
        for t in range(NT):
            for c in range(2):
                last = nc.tensor.transpose(ps[:, 6, t * TOK + c * P:t * TOK + (c + 1) * P],
                                           proj1[:, 2 + c, t * P:(t + 1) * P], ident)
        last.then_inc(vtr1_ready, 1)
        pe.wait_ge(rope_done, 14)
        pe.wait_ge(kdup_evac, KV_HEADS)
        pe.wait_ge(vn1_ready, 1)
        attention(1)
        pe.wait_ge(o_evac, 16)
        n_stage(2, P_OUT1, S_OUT + S_EXP, S_OUT)
        to_dims(2)
        t_stage(P_WQ1, T_WQ1, S_WQ, 5)
        experts(1, P_U1, P_V1, T_U1)
        to_dims(3)

    @block.vector
    def _(dve):
        own = Chain(dve, dve_own, dve_settled)
        v = nc.vector

        def lo(p, j):
            dve.wait_ge(hi_ready, p + 1)
            v.tensor_tensor(wl[:, j, :], raw[:, j, :], wh[:, j, :].bitcast(F32), ALU.subtract).then_inc(lo_ready, 1)

        def ahead(p0):
            for n in range(AHEAD):
                lo(p0 + n, n)

        def split_t(p0, n, done=0):
            if done:
                for j in range(done, RING):
                    lo(p0 + j, j)
            with dve.Fori(1 if done else 0, 2 * n // RING) as i:
                for j in range(RING):
                    lo(i * RING + (p0 + j), j)

        def low_x(src, n):
            for q in range(QX):
                low_quarter(src, n, q)

        def low_quarter(src, n, q):
            part = slice(q * CQ, (q + 1) * CQ)
            dve.wait_ge(xh_ready, QX * n + q + 1)
            v.tensor_tensor(xl[:, part, :], src[:, part, :], xh[:, part, :].bitcast(F32), ALU.subtract)\
                .then_inc(x_ready, 1)

        def act_low(src, chunk, s):
            dve.wait_ge(acth_ready, chunk + 1)
            v.tensor_tensor(act_l[:, s, :], src, act_h[:, s, :].bitcast(F32), ALU.subtract).then_inc(actl_ready, 1)

        def split_n(p0, c0, n, source):
            with dve.Fori(0, n // 2) as i:
                for s in range(2):
                    for e in range(2):
                        lo(i * RING + (p0 + 2 * s + e), 2 * s + e)
                    act_low(source(i, s), i * 2 + (c0 + s), s)

        def attention(layer):
            n0, groups = ATT0[layer], ATT[layer]

            def top(g):
                swa, c = groups[g]
                s, bank = (n0 + g) % 3, 2 * ((n0 + g) % 2)
                dve.wait_ge(s_ready, n0 + g + 1)
                if g >= 3:
                    dve.wait_ge(pt_ready, n0 + g - 2)
                banks = ps[:, bank:bank + 2, :]
                flat = ssb[:, s, :, :].rearrange("p (a b) c -> p a (b c)", a=2)
                mx, negm, es, sd = (asm[:, s, k, :] for k in (0, 1, 3, 4))
                if swa:
                    mask = rcon[:, 3:7, :].rearrange("p a b -> p (a b)").unsqueeze(1).broadcast_to([P, 2, 2 * TOK])
                    own.link(v.scalar_tensor_tensor(out=flat, in0=banks, scalar=64 ** -0.5, in1=mask,
                                                    op0=ALU.mult, op1=ALU.add))
                else:
                    own.link(v.tensor_scalar(flat, banks, MEM_D ** -0.5, None, ALU.mult))
                own.link(v.tensor_reduce(mx, ssb[:, s, :, :], AX.X, ALU.max))
                if swa:
                    sink = par[:, R_SINK + 2 * c:R_SINK + 2 * c + 2].unsqueeze(2).broadcast_to([P, 2, 2])
                    mx2, sd2 = (m.rearrange("p (a b) -> p a b", a=2) for m in (mx, sd))
                    own.link(v.tensor_tensor(mx2, mx2, sink, ALU.max))
                    own.mark(v.tensor_tensor(sd2, sink, mx2, ALU.subtract))
                    own.sync()
                v.tensor_scalar(negm, mx, -1.0, None, ALU.mult).then_inc(negm_ready, 1)

            def normalise(g):
                swa, c = groups[g]
                s = (n0 + g) % 3
                den, es = asm[:, s, 2, :], asm[:, s, 3, :]
                dve.wait_ge(p_ready, n0 + g + 1)
                dve.wait_ge(act_own, att_own(layer, g))
                if swa:
                    own.link(v.tensor_tensor(den, den, es, ALU.add))
                own.link(v.reciprocal(den, den))
                v.tensor_tensor(ssb[:, s, :, :], ssb[:, s, :, :], den.unsqueeze(2).broadcast_to([P, 4, TOK]),
                                ALU.mult).then_inc(pn_ready, 1)

            top(0)
            for g in range(len(groups)):
                if g + 1 < len(groups):
                    top(g + 1)
                normalise(g)

        def att_own(layer, g):
            n = 1 + 2 * SSM_HEADS
            for l, groups in enumerate(ATT):
                for k, (swa, _) in enumerate(groups):
                    n += 4 if swa else 3
                    if (l, k) == (layer, g):
                        return n

        def alpha(n):
            v.tensor_scalar(alf, ident, ALPHA, None, ALU.mult).then_inc(alf_ready, 1)
            dve.wait_ge(al_h_ready, n + 1)
            v.tensor_tensor(al_c[:, 1, :], alf, al_c[:, 0, :].bitcast(F32), ALU.subtract).then_inc(al_ready, 1)

        def norm(n, p_end, p_next):
            if n < 3:
                ahead(p_next)
            dve.wait_ge(piece_used, p_end)
            for t in range(NT):
                for q in range(4):
                    own.mark(v.bn_stats(out=lnst[:, t, q, :], in_=ps[:, 4 * t + q, :]))
                own.sync()
                own.mark(v.bn_aggr(out=lnmv[:, t, 0:2], in_=lnst[:, t, :, :].rearrange("p a b -> p (a b)")))
            own.sync()
            v.tensor_scalar(lnmv[:, :, 5:6], lnmv[:, :, 0:1], -1.0, None, ALU.mult).then_inc(var_ready, 1)
            dve.wait_ge(std_ready, n + 1)
            own.link(v.reciprocal(lnmv[:, :, 3:4], lnmv[:, :, 2:3]))
            dve.wait_ge(var_ready, n + 1)
            v.tensor_tensor(lnmv[:, :, 4:5], lnmv[:, :, 5:6], lnmv[:, :, 3:4], ALU.mult).then_inc(rstd_ready, 1)
            v.tensor_scalar(xn[:, 1, :], ps[:, 4:8, :].rearrange("p a b -> p (a b)"), lnmv[:, 1, 0:1],
                            lnmv[:, 1, 3:4], ALU.subtract, ALU.mult).then_inc(xn_ready, 1)
            for q in range(QX):
                b = 2 * q + 1
                dve.wait_ge(xtr_ready, 8 * n + b + 1)
                for c in (2 * b, 2 * b + 1):
                    gain, shift = C_LN + 2 * n * KC + c, C_LN + (2 * n + 1) * KC + c
                    v.tensor_scalar(xt[:, c, :], ps[:, b, (c % 2) * TOK:(c % 2 + 1) * TOK], par[:, gain:gain + 1],
                                    par[:, shift:shift + 1], ALU.mult, ALU.add).then_inc(xtd_ready, 1)
                if n < 3 and q >= 1:
                    low_quarter(xt, n + 2, q - 1)
            if n < 3:
                low_quarter(xt, n + 2, QX - 1)

        def experts(layer, u0, v0, c0):
            for b in range(UNITS // 4):
                dve.wait_ge(sc_ready, 4 * layer + b + 1)
                bank = 2 + 2 * (b % 3)
                v.tensor_copy(sc[:, 4 * b:4 * b + 4, :, :].rearrange("p u t k -> p t u k"),
                              ps[:, bank:bank + 2, :].rearrange("p t (u k) -> p t u k", u=4)).then_inc(sc_evac, 1)
            dve.wait_ge(sc_evac, 4 * layer + 4)

            s0, s1 = sw[:, 0], sw[:, 1]
            sums, left = (cand[:, k].rearrange("p a b -> p (a b)") for k in range(2))
            pairs = pick.rearrange("p (w k) a -> p w k a", w=2)

            def unit(i, head=True, tail=True):
                def low(n):
                    if head:
                        lo(i * (2 * BODY) + (u0 + n), n % RING)
                    own.sync()

                if head:
                    own.mark(v.tensor_copy(s0, sc[:, i, :, :]))
                if tail:
                    own.mark(v.max_index(best_i[:, 0, 8:16], best_v[:, 8:16], left))
                low(0)
                if tail:
                    own.mark(v.tensor_scalar(best_i[:, 1, :], best_i[:, 0, :], 4, None, ALU.logical_shift_right))
                    own.mark(v.tensor_scalar(best_i[:, 2, :], best_i[:, 0, :], TOPK - 1, None, ALU.bitwise_and))
                if head:
                    for t in range(2):
                        own.mark(v.max(top_v[:, t, 0:8], s0[:, t, :]))
                low(1)
                if tail:
                    own.mark(v.tensor_copy(best_f, best_i[:, 1:3, :]))
                    own.mark(v.tensor_scalar(sel[:, 2, bass.ds((i - 1) * TOPK, TOPK)], best_v, best_v[:, 0:1], None,
                                             ALU.subtract))
                if head:
                    for t in range(2):
                        own.mark(v.max_index(top_i[:, t, 0:8], top_v[:, t, 0:8], s0[:, t, :]))
                        own.mark(v.match_replace(out=s1[:, t, :], in_to_replace=top_v[:, t, 0:8],
                                                 in_values=s0[:, t, :], imm_value=NEG))
                low(2)
                if tail:
                    own.mark(v.tensor_tensor(pick, best_f.rearrange("p w k -> p (w k)").unsqueeze(2)
                                             .broadcast_to([P, 2 * TOPK, TOPK]),
                                             iota[:, 0:TOPK].unsqueeze(1).broadcast_to([P, 2 * TOPK, TOPK]),
                                             ALU.is_equal))
                if head:
                    for t in range(2):
                        own.mark(v.max(top_v[:, t, 8:16], s1[:, t, :]))
                low(3)
                if tail:
                    own.mark(v.tensor_tensor(pairs, pairs, top_f.unsqueeze(2).broadcast_to([P, 2, TOPK, TOPK]),
                                             ALU.mult))
                if head:
                    own.mark(v.tensor_tensor(cand[:, 0], top_v[:, 0, :].unsqueeze(2).broadcast_to([P, TOPK, TOPK]),
                                             top_v[:, 1, :].unsqueeze(1).broadcast_to([P, TOPK, TOPK]), ALU.add))
                    for t in range(2):
                        own.mark(v.max_index(top_i[:, t, 8:16], top_v[:, t, 8:16], s1[:, t, :]))
                low(4)
                if tail:
                    own.mark(v.tensor_reduce(sel[:, 0:2, bass.ds((i - 1) * TOPK, TOPK)], pairs, AX.X, ALU.add))
                if head:
                    own.mark(v.max(best_v[:, 0:8], sums))
                low(5)
                if head:
                    own.mark(v.tensor_copy(top_f, top_i))
                    own.mark(v.max_index(best_i[:, 0, 0:8], best_v[:, 0:8], sums))
                    own.mark(v.match_replace(out=left, in_to_replace=best_v[:, 0:8], in_values=sums, imm_value=NEG))
                    lo(i * (2 * BODY) + (u0 + 6), 6 % RING)
                    own.sync()
                    lo(i * (2 * BODY) + (u0 + 7), 7 % RING)
                    own.mark(v.max(best_v[:, 8:16], left))
                    own.sync()

            unit(0, tail=False)
            with dve.Fori(1, TRIPS) as i:
                own.enter(i, 1, 25)
                unit(i)
            own.leave(TRIPS - 1)
            unit(TRIPS, head=False)
            own.sync()
            v.tensor_copy(gsm[:, 0, 0:1], iota[:, 0:1]).then_inc(gd_ready, 1)
            dve.wait_ge(ge_ready, layer + 1)
            gates = sel[:, 2, :].rearrange("p (u k) -> p u k", k=TOPK)
            own.link(v.tensor_reduce(gsm[:, 0, :], gates, AX.X, ALU.add))
            own.link(v.reciprocal(gsm[:, 1, :], gsm[:, 0, :]))
            v.tensor_tensor(gates, gates, gsm[:, 1, :].unsqueeze(2).broadcast_to([P, UNITS, TOPK]),
                            ALU.mult).then_inc(sel_ready, 1)
            dve.wait_ge(selt_evac, 3 * layer + 3)

            def spread(i):
                for s in range(BODY):
                    q = (i - TRIPS) * 4 + s
                    for e in range(2):
                        lo(i * (2 * BODY) + (u0 + 2 * s + e), (2 * s + e) % RING)

                    def of(w):
                        return sel_t[:, w, bass.ds(q * 4, 4)].unsqueeze(2).broadcast_to([P, 4, P])
                    rows = iota.unsqueeze(1).broadcast_to([P, 4, P])
                    if not isinstance(q, int) or layer or q >= 1:
                        dve.wait_ge(g_ready, q + layer * TOK // 4)
                    own.mark(v.tensor_tensor(hot[:, 1], rows, of(0), ALU.is_equal))
                    own.mark(v.tensor_tensor(hot[:, 0], rows, of(1), ALU.is_equal))
                    own.sync()
                    v.tensor_tensor(hot[:, 1], hot[:, 1], of(2), ALU.mult).then_inc(hot_ready, 1)

            spread(TRIPS)
            with dve.Fori(TRIPS + 1, 2 * TRIPS) as i:
                own.enter(i, TRIPS + 1, 8)
                spread(i)
            own.leave(TRIPS - 1)
            alpha(2 * layer + 1)
            dve.wait_ge(g_evac, (layer + 1) * TOK // 4)
            with dve.Fori(0, S_EXP // BODY) as i:
                for k in range(BODY):
                    s = k % 2
                    n = i * BODY + (layer * S_EXP + k)
                    dve.wait_ge(h_loaded[k], i * 16 + 16 * (layer * (S_EXP // BODY) + 1))
                    dve.wait_ge(actl_ready, i * BODY + (c0 + k - 1))
                    v.tensor_tensor(act_t[:, s, :], hring[:, k, :], gate_of[:, i * BODY + k, :],
                                    ALU.mult).then_inc(act_ready, 1)
                    for e in range(2):
                        lo(i * (2 * BODY) + (v0 + 2 * k + e), (2 * k + e) % RING)
                    dve.wait_ge(act_ready, n + 1)
                    act_low(act_t[:, s, :], i * BODY + (c0 + k), s)

        v.memset(epsc, LN_EPS).then_inc(eps_set, 1)
        low_x(in_raw, 0)
        split_t(P_MEM, S_MEM)
        low_x(in_raw, 1)
        own.mark(v.memset(lcon[:, 2, :], 1.0 / (GC * P)))
        dve.wait_ge(spill_done, 32)
        dve.wait_ge(vn_ready, 5)
        own.mark(v.memset(proj[:, 0:XBC_C, 0:LPAD], 0.0))
        dve.wait_ge(consts_in, 48)
        dve.wait_ge(l0_in, 32)
        own.mark(v.tensor_copy(ident_b, ident))
        own.mark(v.tensor_scalar(later_b, lcon[:, 1, :], MASKED, None, ALU.mult))
        own.mark(v.tensor_copy(tri_r[:, 0, :], lcon[:, 0, :]))
        own.mark(v.tensor_copy(tri_r[:, 1, :], lcon[:, 0, :]))
        split_t(P_INA, XBC_C)

        dve.wait_ge(dt_ready, 1)
        raw_dt = ps[:, 7, 0:48].rearrange("p (t h) -> p t h", t=NT)
        row = lambda k: dts[:, k, :].rearrange("p (t h) -> p t h", t=NT)
        own.link(v.tensor_tensor(row(0), raw_dt, par[:, R_DTB:R_DTB + 24].unsqueeze(1).broadcast_to([P, NT, 24]), ALU.add))
        own.link(v.tensor_scalar(dts[:, 9, :], dts[:, 0, :], -1.0, None, ALU.mult))
        v.tensor_tensor(dts[:, 1, :], dts[:, 0, :], dts[:, 9, :], ALU.max).then_inc(dtx_ready, 1)
        own.mark(v.tensor_scalar(dts[:, 11, :], dts[:, 0, :], 0.0, None, ALU.max))
        FIVE = XBC_C // 4
        with dve.Fori(0, 4) as i:
            own.enter(i, 0, FIVE * CONV_W)
            dve.wait_ge(evac_done, i * FIVE + (T_INA + FIVE))
            for k in range(CONV_W):
                own.sync()
                for m in range(FIVE):
                    c = i * FIVE + m
                    src = proj[:, c, k:k + TOK]
                    wk = par[:, bass.ds(c * CONV_W + (C_CONVW + k), 1)]
                    if k == 0:
                        own.mark(v.tensor_scalar(xc[:, c, :], src, wk, par[:, bass.ds(c + C_CONVB, 1)],
                                                 ALU.mult, ALU.add))
                    else:
                        own.mark(v.scalar_tensor_tensor(out=xc[:, c, :], in0=src, scalar=wk, in1=xc[:, c, :],
                                                        op0=ALU.mult, op1=ALU.add))
                for j in (2 * k, 2 * k + 1):
                    lo(i * (2 * BODY) + (P_INA + 2 * XBC_C + j), j % RING)
        own.leave(4)
        own.sync()
        v.tensor_copy(dts[:, 10, 0:1], iota[:, 0:1]).then_inc(conv_done, 1)

        dve.wait_ge(dtl_ready, 1)
        dve.wait_ge(dte_ready, 1)
        own.link(v.tensor_tensor(dts[:, 5, :], dts[:, 11, :], dts[:, 3, :], ALU.add))
        own.link(v.tensor_scalar(dts[:, 4, 24:48], dts[:, 4, 0:24], -1.0, None, ALU.mult))
        v.tensor_tensor(row(6), row(5), dts[:, 4, 24:48].unsqueeze(1).broadcast_to([P, NT, 24]), ALU.mult)\
            .then_inc(adt_ready, 1)
        dve.wait_ge(adth_ready, 1)
        v.tensor_tensor(adt_r[:, 1, :], dts[:, 6, :], adt_r[:, 0, :].bitcast(F32), ALU.subtract).then_inc(adtr_ready, 1)
        for g in range(GROUPS):
            dve.wait_ge(cbo_ready, g + 1)
            v.tensor_tensor(cbm[:, g, :].rearrange("p (a b) -> p a b", a=3)[:, 0:3:2, :],
                            ps[:, 2 + g, 0:384].rearrange("p (a b) -> p a b", a=3)[:, 0:3:2, :],
                            lcon[:, 0, :].unsqueeze(1).broadcast_to([P, 2, P]), ALU.mult).then_inc(cbm_ready, 1)
        dve.wait_ge(cs_ready, 1)
        own.mark(v.tensor_scalar(dts[:, 7, :], ps[:, 6, 0:48], -1.0, None, ALU.mult))
        own.sync()
        v.tensor_copy(dts[:, 8, 0:24], ps[:, 6, 64:88]).then_inc(cs_evac, 1)
        for b in range(6):
            dve.wait_ge(xst_ready, b + 1)
            for t in range(NT):
                ins = v.tensor_tensor(
                    xdt[:, t, 4 * b:4 * b + 4, :].rearrange("p (c h) d -> p c h d", c=2),
                    ps[:, b, :].rearrange("p (c t h d) -> p c t h d", c=2, t=2, h=2)[:, :, t, :, :],
                    dts[:, 5, t * 24 + 4 * b:t * 24 + 4 * b + 4].rearrange("p (c h) -> p c h", c=2)
                    .unsqueeze(3).broadcast_to([P, 2, 2, 64]), ALU.mult)
                if t == 0:
                    own.mark(ins)
                else:
                    own.sync()
                    ins.then_inc(xdt_ready, 1)

        dve.wait_ge(cbo_ready, GROUPS)
        dve.wait_ge(cbm_ready, GROUPS)
        dve.wait_ge(silu_done, 3)

        def gate_y(c):
            dve.wait_ge(y_ready, 2 * c + 2)
            own.link(v.scalar_tensor_tensor(out=cat[:, c, :], in0=xc[:, c, :],
                                            scalar=par[:, C_DSKIP + c:C_DSKIP + c + 1], in1=ps[:, c % 2, 0:TOK],
                                            op0=ALU.mult, op1=ALU.add))
            v.tensor_tensor(cat[:, c, :], cat[:, c, :], proj[:, XBC_C + c, LPAD:LPAD + TOK],
                            ALU.mult).then_inc(y_done, 1)

        for h in range(SSM_HEADS):
            s, c = h % 2, h // 2
            dve.wait_ge(ex_ready, h + 1)
            dve.wait_ge(act_own, 1 + 2 * (h + 1))
            if h >= 2:
                dve.wait_ge(y_ready, h - 1)
            v.tensor_tensor(mt[:, s, :], ex[:, s, :], cbm[:, h // 6, :], ALU.mult).then_inc(m_ready, 1)
            if h % 2 and c >= 1:
                gate_y(c - 1)
        gate_y(MC - 1)
        for g in range(GROUPS):
            dve.wait_ge(rms_ready, g + 1)
            own.link(v.reciprocal(nrm[:, g, :], nrm[:, g, :]))
            for c in range(g * GC, (g + 1) * GC):
                ins = v.scalar_tensor_tensor(out=cat[:, c, :], in0=cat[:, c, :],
                                             scalar=par[:, C_NORMG + c:C_NORMG + c + 1], in1=nrm[:, g, :],
                                             op0=ALU.mult, op1=ALU.mult)
                own.mark(ins)
        attention(0)
        own.sync()
        v.tensor_copy(dts[:, 10, 0:1], iota[:, 0:1]).then_inc(cat_ready, 1)
        alpha(0)
        dve.wait_ge(o_evac, 2)
        split_n(P_OUT0, 0, S_OUT, lambda i, s: cat[:, i * 2 + s, :])
        norm(0, P_WQ0, P_WQ0)
        split_t(P_WQ0, S_WQ, done=AHEAD)
        experts(0, P_U0, P_V0, S_OUT)
        norm(1, P_INB, P_INB)

        split_t(P_INB, S_INB, done=AHEAD)
        dve.wait_ge(l1_in, 64)
        own.link(v.tensor_copy(ang[:, 2, :], posi))
        own.link(v.tensor_scalar(ang[:, 3, :], ang[:, 2, :], par[:, C_FREQ:C_FREQ + 1], None, ALU.mult))
        for k, (turn, quarter) in enumerate(((0.25, 1.5707963267948966), (0.0, 0.0))):
            own.link(v.tensor_scalar(ang[:, 4, :], ang[:, 3, :], 0.15915494309189535, turn, ALU.mult, ALU.add))
            own.link(v.tensor_scalar(ang[:, 5, :], ang[:, 4, :], 12582912.0, None, ALU.add))
            own.link(v.tensor_scalar(ang[:, 4, :], ang[:, 5, :], -12582912.0, None, ALU.add))
            own.link(v.scalar_tensor_tensor(out=ang[:, 5, :], in0=ang[:, 4, :], scalar=-6.28125, in1=ang[:, 3, :],
                                            op0=ALU.mult, op1=ALU.add))
            own.link(v.scalar_tensor_tensor(out=ang[:, 5, :], in0=ang[:, 4, :], scalar=-0.0019350051879882812,
                                            in1=ang[:, 5, :], op0=ALU.mult, op1=ALU.add))
            own.link(v.scalar_tensor_tensor(out=ang[:, k, :], in0=ang[:, 4, :], scalar=-3.019916050561733e-07,
                                            in1=ang[:, 5, :], op0=ALU.mult, op1=ALU.add))
            own.link(v.tensor_scalar(ang[:, k, :], ang[:, k, :], quarter, 3.1415925, ALU.add, ALU.min))
            ins = v.tensor_scalar(ang[:, k, :], ang[:, k, :], -3.1415925, None, ALU.max)
            if k == 0:
                own.link(ins)
            else:
                ins.then_inc(trig_in, 1)
        dve.wait_ge(cossin_ready, 1)
        dve.wait_ge(evac_done, T_INB + S_INB)
        for n in range(14):
            c = n if n < 2 else n + 2
            own.link(v.tensor_tensor(rtmp[:, n % 2, 0, :], proj1[:, c, :], cs[:, 0, :], ALU.mult))
            dve.wait_ge(rot_ready, n + 1)
            own.link(v.tensor_tensor(rtmp[:, n % 2, 1, :], ps[:, n % 2, 0:TOK], cs[:, 1, :], ALU.mult))
            v.tensor_tensor(proj1[:, c, :], rtmp[:, n % 2, 0, :], rtmp[:, n % 2, 1, :], ALU.add).then_inc(rope_done, 1)
        attention(1)
        alpha(2)
        dve.wait_ge(o_evac, 16)
        split_n(P_OUT1, S_OUT + S_EXP, S_OUT, lambda i, s: cat[:, i * 2 + s, :])
        norm(2, P_WQ1, P_WQ1)
        split_t(P_WQ1, S_WQ, done=AHEAD)
        experts(1, P_U1, P_V1, 2 * S_OUT + S_EXP)
        norm(3, P_END, None)

    block_cm.__exit__(None, None, None)
    for c in reversed(ctxs):
        c.__exit__(None, None, None)


def shape_constants():
    import numpy as np
    k = np.arange(P)
    ident = np.eye(P)
    iota = np.broadcast_to(k, (P, P))
    tri = k[:, None] <= k[None, :]
    strict = k[:, None] > k[None, :]
    rot = np.zeros((P, P))
    for m in range(P):
        rot[m + 32 if m % 64 < 32 else m - 32, m] = -1.0 if m % 64 < 32 else 1.0
    dup = np.zeros((2, P, P))
    for a in range(2):
        for m in range(P):
            dup[a, a * 64 + m % 64, m] = 1.0
    q = np.arange(TOK) // 64
    seen = (q[None, :] == q[:, None]) | (q[None, :] == q[:, None] - 1)
    mask = np.where(seen, 0.0, MASKED).reshape(NT, P, TOK).transpose(1, 0, 2).reshape(P, 4, P)
    f = np.float32
    base = np.stack([ident, iota], 1).astype(f)
    tris = np.stack([tri, strict], 1).astype(f)
    rcon = np.concatenate([np.stack([rot, dup[0], dup[1]], 1), mask], 1).astype(f)
    inv = (f(1.0) / np.power(f(10000.0), np.arange(0, 64, 2, dtype=f) / f(64))).astype(f)
    return base, tris, rcon, inv[k % 32]


def kernel(x, mem, positions, w_in_a, conv_w, conv_b, dt_bias, a_log, d_skip, ssm_norm_g, w_kv_shared, w_in_b,
           attn_sinks, w_mem_kv, w_out, ln_g, ln_b, peer_wq, peer_subkeys, peer_u, peer_v):
    import numpy as np
    import concourse.bacc as bacc
    from concourse.bass_utils import run_bass_kernel_spmd

    def t_slabs(w):
        n = w.shape[1] // P
        a = np.asarray(w).reshape(2, KC // 2, P, n, P)
        return a.transpose(3, 0, 2, 1, 4).reshape(2 * n, P, PC)

    def n_slabs(w):
        n = w.shape[0] // P
        return np.asarray(w).reshape(n, P, 2, PC).transpose(0, 2, 1, 3).reshape(2 * n, P, PC)

    wa, wb, wkv = np.asarray(w_in_a)[0], np.asarray(w_in_b)[0], np.asarray(w_kv_shared)
    conv_dim = XBC_C * P
    o_c, o_d = MAIN, MAIN + conv_dim
    o_m = o_d + SSM_HEADS
    w = np.concatenate([
        t_slabs(np.asarray(w_mem_kv)[0]), t_slabs(np.asarray(w_mem_kv)[1]),
        t_slabs(wa[:, o_c:o_d]), t_slabs(wa[:, :MAIN]), t_slabs(wa[:, o_m:]),
        n_slabs(w_out[0]), t_slabs(np.asarray(peer_wq)[0]),
        t_slabs(wkv), t_slabs(wb), n_slabs(w_out[1]), t_slabs(np.asarray(peer_wq)[1]),
    ])
    u = np.concatenate([t_slabs(np.asarray(peer_u)[l].T) for l in range(2)])
    vv = np.concatenate([n_slabs(peer_v[l]) for l in range(2)])
    base, tris, rcon, freq = shape_constants()

    def cols(a, c):
        return np.asarray(a).reshape(c, P).T

    par_cols = np.concatenate([
        np.asarray(conv_w)[0].reshape(CONV_W, XBC_C, P).transpose(2, 1, 0).reshape(P, -1),
        cols(conv_b[0], XBC_C),
        cols(np.repeat(np.asarray(d_skip)[0], 64), MC),
        cols(ssm_norm_g[0], MC),
        np.stack([np.asarray(ln_g), np.asarray(ln_b)], 2).reshape(8, KC, P).transpose(2, 0, 1).reshape(P, -1),
        freq[:, None],
    ], 1)
    arrays = {
        "w": w, "u": u, "v": vv,
        "base": base, "tri": tris, "rcon": rcon, "cols": par_cols,
        "rows": np.concatenate([np.asarray(dt_bias)[0], np.asarray(a_log)[0], np.asarray(attn_sinks)[0]]),
        "memT": np.asarray(mem)[0].reshape(TOK, KC, P).transpose(2, 1, 0),
        "xT": np.asarray(x)[0].reshape(TOK, KC, P).transpose(2, 1, 0),
        "dtw": wa[:, o_d:o_m].reshape(KC, P, SSM_HEADS).transpose(1, 0, 2),
        "subk": np.asarray(peer_subkeys).transpose(0, 2, 4, 1, 3).reshape(2, P, PEER_H, KEYS),
        "pos": np.asarray(positions)[0],
    }
    arrays = {f"in_{k}": np.ascontiguousarray(a) for k, a in arrays.items()}
    nc = bacc.Bacc("TRN2", target_bir_lowering=False, num_devices=1, dynamic_dma_scratch_size=64)
    dram = {}
    for k, a in arrays.items():
        dram[k[3:]] = nc.dram_tensor(k, a.shape, mybir.dt.from_np(a.dtype), kind="ExternalInput").ap()
    dram["out"] = nc.dram_tensor("out_x", (P, KC, TOK), F32, kind="ExternalOutput").ap()
    dram["h"] = nc.dram_tensor("h_scratch", (S_EXP, P, TOK), F32, kind="Internal").ap()
    dram["spill"] = nc.dram_tensor("kv_scratch", (P, 2048), F32, kind="Internal").ap()
    build(nc, dram)
    r = run_bass_kernel_spmd(nc, [arrays], core_ids=[0])
    got = r.results[0]["out_x"]
    return np.ascontiguousarray(got.transpose(2, 1, 0).reshape(1, TOK, D))
```

```python
import concourse.bass as bass
from concourse import mybir

F32 = mybir.dt.float32
F32R = mybir.dt.float32r
U32 = mybir.dt.uint32
I32 = mybir.dt.int32
BF16 = mybir.dt.bfloat16
ALU = mybir.AluOpType
ACT = mybir.ActivationFunctionType
AX = mybir.AxisListType

P = 128
TOK = 256
NT = TOK // P
D = 2048
KC = D // P
PC = D // 2
RING = 4
QX = 4
CQ = KC // QX
AHEAD = 3
MEM_HEADS, MEM_D = 4, 128
MAIN = 1536
MC = MAIN // P
GROUPS = 4
GC = MC // GROUPS
SSM_HEADS = 24
CONV_W = 4
XBC_C = 20
ATT_HEADS = 24
KV_HEADS = 4
PEER_H = 8
KEYS = 128
TOPK = 16
UNITS = NT * PEER_H
PITCH = TOK + 4
LPAD = CONV_W - 1
ALPHA = 4.0 ** 0.25
EPS = 1e-5
NEG = -3.0e38
MASKED = -1.0e30

S_MEM, S_INA, S_OUT, S_WQ, S_EXP, S_INB = 16, 36, KC, PEER_H, KEYS, 20
P_MEM = 0
P_INA = P_MEM + 2 * S_MEM
P_OUT0 = P_INA + 2 * S_INA
P_WQ0 = P_OUT0 + 2 * S_OUT
P_U0 = P_WQ0 + 2 * S_WQ
P_V0 = P_U0 + 2 * S_EXP
P_INB = P_V0 + 2 * S_EXP
P_OUT1 = P_INB + 2 * S_INB
P_WQ1 = P_OUT1 + 2 * S_OUT
P_U1 = P_WQ1 + 2 * S_WQ
P_V1 = P_U1 + 2 * S_EXP
P_END = P_V1 + 2 * S_EXP
T_MEM = 0
T_INA = T_MEM + S_MEM
T_WQ0 = T_INA + S_INA
T_U0 = T_WQ0 + S_WQ
T_INB = T_U0 + S_EXP
T_WQ1 = T_INB + S_INB
T_U1 = T_WQ1 + S_WQ

C_CONVW, C_CONVB = 0, XBC_C * CONV_W
C_DSKIP = C_CONVB + XBC_C
C_NORMG = C_DSKIP + MC
C_LN = C_NORMG + MC
C_FREQ = C_LN + 4 * 2 * KC
C_COLS = C_FREQ + 1
R_DTB, R_ALOG, R_SINK = C_COLS, C_COLS + 24, C_COLS + 48
R_EPS = C_COLS + 72
PAR = R_EPS + 1

K_IDENT, K_IOTA, K_TRI, K_STRICT = 0, 128, 256, 384
K_ROT, K_DUP, K_MASK = 512, 640, 896
K_COLS = K_MASK + 512

BODY = 4
ROUTE = 6
SPREAD0 = UNITS * ROUTE // BODY
TRIPS_E = S_EXP // BODY
Q_TRIP = TOK // 4 // (TRIPS_E - SPREAD0)
HOUT = 2
assert UNITS * ROUTE == SPREAD0 * BODY and Q_TRIP == 2 * BODY


class Chain:

    def __init__(self, eng, sem, settled=None):
        self.settled = settled
        self.eng, self.sem, self.n, self.loop = eng, sem, 0, None

    def value(self):
        if self.loop is None:
            return self.n
        i, start, per, base = self.loop
        return (i - start) * per + (base + self.n)

    def mark(self, ins):
        ins.then_inc(self.sem, 1)
        self.n += 1

    def sync(self):
        self.eng.wait_ge(self.sem, self.value())

    def settle(self):
        self.sync()
        self.eng.sem_inc(self.settled, 1)

    def settle_link(self, ins):
        self.mark(ins)
        self.settle()

    def link(self, ins):
        self.mark(ins)
        self.sync()

    def enter(self, i, start, per):
        self.loop = (i, start, per, self.n)
        self.n = 0

    def leave(self, trips):
        _, _, per, base = self.loop
        assert self.n == per, self.n
        self.loop, self.n = None, base + per * trips


def build(nc, dram):
    ctxs = []

    def sem(name):
        c = nc.semaphore(name)
        ctxs.append(c)
        return c.__enter__()

    at = [(nc.sbuf_base + 31) // 32 * 32]

    def sb(name, shape, dt, offset=None):
        size = 4
        for n in shape[1:]:
            size *= n
        if offset is None:
            offset = at[0]
            at[0] += (size + 31) // 32 * 32
        return nc.alloc_sbuf_tensor_at(name, shape, dt, offset=offset)

    arena_at = at[0]
    arena = sb("arena", [P, S_EXP * TOK], F32)
    xh = sb("xh", [P, KC, TOK], F32R)
    xl = sb("xl", [P, KC, TOK], F32R)
    raw = sb("raw", [P, RING, PC], F32)
    wh = sb("wh", [P, RING, PC], F32R)
    wl = sb("wl", [P, RING, PC], F32R)
    hring = sb("hring", [P, BODY, TOK], F32)
    act_at = at[0]
    act_t = sb("act_t", [P, 2, TOK], F32)
    act_h = sb("act_h", [P, 2, TOK], F32R)
    act_l = sb("act_l", [P, 2, TOK], F32R)
    hot = sb("hot", [P, 2, 2, 4, P], F32, offset=act_at - (BODY - HOUT) * TOK * 4)
    sel_at = at[0]
    sel_t = sb("sel_t", [P, 3, TOK], F32)
    base_c = sb("base_c", [P, 2, P], F32)
    par = sb("par", [P, PAR], F32)
    assert at[0] <= nc.sbuf_usable_end, at[0]
    ident, iota = base_c[:, 0, :], base_c[:, 1, :]
    epsc = par[:, R_EPS:R_EPS + 1]

    def A(off, *shape, dt=F32):
        n = 1
        for k in shape:
            n *= k
        assert off + n <= S_EXP * TOK
        v = arena[:, off:off + n]
        if dt is not F32:
            v = v.bitcast(dt)
        names = "abcd"[:len(shape)]
        if len(shape) == 1:
            return v
        return v.rearrange(f"p ({' '.join(names)}) -> p {' '.join(names)}",
                           **{c: k for c, k in zip(names[1:], shape[1:])})

    psc = nc.psum_tensor("ps", [P, 8, 512], F32)
    ctxs.append(psc)
    ps = psc.__enter__()

    proj = A(0, S_INA, PITCH)
    xc = A(9360, XBC_C, TOK)
    cat = A(14480, KC, TOK)
    kvt = A(18576, 8, TOK)
    vn = A(20624, 2, 512)
    in_raw = A(24464, KC, TOK)
    xdt = A(21648, NT, SSM_HEADS, 64)
    cbm = A(24720, GROUPS, 384)
    ex = A(27024, 2, 384)
    mt = A(27792, 2, 384)
    lcon = A(28560, 3, P)
    dtw = A(28944, KC, SSM_HEADS)
    dts = A(29328, 12, 48)
    nrm = A(29904, 4, TOK)
    ysq = A(0, 2, GC, TOK)
    tri_r = nc.alloc_sbuf_tensor_at("tri_r", [P, 2, P], F32R, offset=arena_at + 4 * 31000)
    adt_r = nc.alloc_sbuf_tensor_at("adt_r", [P, 2, 48], F32R, offset=arena_at + 4 * 31256)
    dtw_f = nc.alloc_sbuf_tensor_at("dtw_r", [P, (KC + 2) * 2 * SSM_HEADS], F32R, offset=arena_at + 4 * 31488)
    dtw_r = dtw_f[:, :].rearrange("p (c w h) -> p c w h", w=2, h=SSM_HEADS)
    dt_c = A(29904, TOK)
    ident_b, later_b = A(31360, P // 2, dt=BF16), A(31424, P // 2, dt=BF16)
    ssb = A(0, 3, 4, TOK)
    pt = A(3072, 2, 2, 2, TOK)
    asm = A(5120, 3, 5, 4)
    proj1 = A(9360, S_INB, TOK)
    kdup = A(21648, KV_HEADS, TOK)
    vn1 = A(22672, NT, TOK)
    rcon = A(23184, 7, P)
    cs = A(24080, 2, TOK)
    rtmp = A(24592, 2, 2, TOK)
    posi = A(25616, TOK, dt=I32)
    ang = A(25872, 6, TOK)
    kvt_all = A(0, S_MEM, TOK)
    vn_spill = A(4096, 2, 512)
    xn = A(0, NT, D)
    xt = A(4096, KC, TOK)
    lnst = A(20200, NT, 4, 6)
    lnmv = A(20300, NT, 8)
    sc = A(0, UNITS, 2, KEYS)
    qt = A(8192, PEER_H, TOK)
    subk = A(10240, PEER_H, KEYS)
    sw = A(11264, 2, 2, KEYS)
    top_v = A(11776, 2, TOPK)
    top_i = A(11808, 2, TOPK, dt=U32)
    top_f = A(11840, 2, TOPK)
    cand = A(11872, 2, TOPK, TOPK)
    best_v = A(12384, TOPK)
    best_i = A(12400, 3, TOPK, dt=U32)
    best_f = A(12448, 2, TOPK)
    pick = A(12480, 2 * TOPK, TOPK)
    sel = A(12992, 3, UNITS * TOPK)
    gsm = A(13760, 2, UNITS)
    gate_of = A(0, KEYS, TOK)
    ident_r = sb("ident_r", [P, P], F32R)[:, :]

    raw_full = [sem(f"raw_full{j}") for j in range(RING)]
    hi_ready, lo_ready, piece_used = sem("hi_ready"), sem("lo_ready"), sem("piece_used")
    evac_done = sem("evac_done")
    consts_in, l0_in, subk_in, l1_in = (sem(n) for n in ("consts_in", "l0_in", "subk_in", "l1_in"))
    memx_in = [sem(f"memx_in{q}") for q in range(QX)]
    eps_set = sem("eps_set")
    xh_ready, x_ready = sem("xh_ready"), sem("x_ready")
    vtr_ready, vn_ready, spill_done = sem("vtr_ready"), sem("vn_ready"), sem("spill_done")
    conv_done, silu_done = sem("conv_done"), sem("silu_done")
    dt_ready, dtx_ready, dte_ready, dtl_in, dtl_ready = (
        sem(n) for n in ("dt_ready", "dtx_ready", "dte_ready", "dtl_in", "dtl_ready"))
    adt_ready, cs_ready, cs_evac = sem("adt_ready"), sem("cs_ready"), sem("cs_evac")
    cb_ready, cbm_ready = sem("cb_ready"), sem("cbm_ready")
    cbo_ready = sem("cbo_ready")
    xst_ready, xdt_ready = sem("xst_ready"), sem("xdt_ready")
    row_ready, ex_ready, m_ready = (sem(n) for n in ("row_ready", "ex_ready", "m_ready"))
    dtwh_ready, dtw_ready = sem("dtwh_ready"), sem("dtw_ready")
    dtc_ready, dtc_evac = sem("dtc_ready"), sem("dtc_evac")
    adth_ready, adtr_ready = sem("adth_ready"), sem("adtr_ready")
    y_ready, y_done = sem("y_ready"), sem("y_done")
    ysq_ready, ms_ready, rms_ready, cat_ready = (sem(n) for n in ("ysq_ready", "ms_ready", "rms_ready", "cat_ready"))
    s_ready, negm_ready, p_ready, pn_ready = (sem(n) for n in ("s_ready", "negm_ready", "p_ready", "pn_ready"))
    pt_ready, pt_evac, o_ready, o_evac = (sem(n) for n in ("pt_ready", "pt_evac", "o_ready", "o_evac"))
    acth_ready, actl_ready, act_ready = sem("acth_ready"), sem("actl_ready"), sem("act_ready")
    ident_ready = sem("ident_ready")
    var_ready, std_ready, rstd_ready = sem("var_ready"), sem("std_ready"), sem("rstd_ready")
    xn0_ready, xn1_ready = sem("xn0_ready"), sem("xn1_ready")
    xtr_ready, xta_ready = sem("xtr_ready"), sem("xta_ready")
    xtd_ready = sem("xtd_ready")
    sc_ready, sc_evac = sem("sc_ready"), sem("sc_evac")
    gd_ready, ge_ready, sel_ready, selt_ready, selt_evac = (
        sem(n) for n in ("gd_ready", "ge_ready", "sel_ready", "selt_ready", "selt_evac"))
    hot_ready, g_ready, g_evac = sem("hot_ready"), sem("g_ready"), sem("g_evac")
    h_stored = [sem(f"h_stored{j}") for j in range(HOUT)]
    h_loaded = [sem(f"h_loaded{j}") for j in range(BODY)]
    trig_in, trig_ready, cossin_ready = sem("trig_in"), sem("trig_ready"), sem("cossin_ready")
    rot_ready, rope_done, kdup_ready, kdup_evac = (sem(n) for n in ("rot_ready", "rope_done", "kdup_ready", "kdup_evac"))
    vtr1_ready, vn1_ready = sem("vtr1_ready"), sem("vn1_ready")
    out_done = sem("out_done")
    act_own, dve_own, dve_settled = sem("act_own"), sem("dve_own"), sem("dve_settled")

    w_in, u_in, v_in = dram["w"], dram["u"], dram["v"]
    h_dram, spill = dram["h"], dram["spill"]

    ATT = [[(0, m) for m in range(2)], [(1, c) for c in range(MC)] + [(0, m) for m in range(2)]]
    ATT0 = [0, 2]
    block_cm = nc.Block()
    block = block_cm.__enter__()

    @block.sync
    def _(sp):
        def piece(src, row, p, j, first=False):
            if not first:
                sp.wait_ge(lo_ready, p - (RING - 1))
            sp.dma_start(raw[:, j, :], src[row, :, :]).then_inc(raw_full[j], 16)

        def stream(src, row0, p0, n):
            with sp.Fori(0, n // RING) as i:
                for j in range(RING):
                    piece(src, i * RING + (row0 + j), i * RING + (p0 + j), j)

        def load_x(name, q):
            sp.dma_start(in_raw[:, q * CQ:(q + 1) * CQ, :], dram[name][:, q * CQ:(q + 1) * CQ, :])\
                .then_inc(memx_in[q], 16)

        for q in range(QX):
            load_x("memT", q)
            piece(w_in, q, q, q, first=True)
        for dst, name in ((base_c[:, :, :], "base"), (par[:, 0:C_COLS], "cols")):
            sp.dma_start(dst, dram[name]).then_inc(consts_in, 16)
        sp.dma_start(par[:, C_COLS:R_EPS], dram["rows"].partition_broadcast(P)).then_inc(consts_in, 16)
        sp.dma_start(lcon[:, 0:2, :], dram["tri"]).then_inc(l0_in, 16)
        sp.dma_start(dtw[:, :, :], dram["dtw"]).then_inc(l0_in, 16)
        stream(w_in, RING, RING, 2 * S_MEM - RING)
        for q in range(QX):
            sp.wait_ge(x_ready, q + 1)
            load_x("xT", q)
        sp.wait_ge(vn_ready, 4)
        sp.dma_start(spill[:, 0:1024], kvt_all[:, 8:12, :]).then_inc(spill_done, 16)
        sp.dma_start(spill[:, 1024:2048], vn_spill[:, :, :]).then_inc(spill_done, 16)
        stream(w_in, P_INA, P_INA, 2 * (S_INA + S_OUT + S_WQ))

        def experts(layer, u0, v0):
            row0 = layer * 2 * S_EXP
            sp.wait_ge(x_ready, QX * (3 if layer == 0 else 5))
            sp.dma_start(subk[:, :, :], dram["subk"][layer, :, :, :]).then_inc(subk_in, 16)

            def store(k, j):
                sp.wait_ge(evac_done, k + ((T_U0, T_U1)[layer] + 1))
                sp.dma_start(h_dram[k, :, :], hring[:, j % HOUT, :]).then_inc(h_stored[j % HOUT], 16)

            def u_trip(i, first):
                for j in range(BODY):
                    for n in (2 * j, 2 * j + 1):
                        piece(u_in, i * (2 * BODY) + (row0 + n), i * (2 * BODY) + (u0 + n), n % RING)
                    if not first or j == BODY - 1:
                        store(i * BODY + (j - 3), j + 1)

            u_trip(0, True)
            with sp.Fori(1, TRIPS_E) as i:
                u_trip(i, False)
            for k in range(S_EXP - 3, S_EXP):
                store(k, k)
            for n in range(RING):
                piece(v_in, row0 + n, v0 + n, n)
            for j in range(HOUT):
                sp.wait_ge(h_stored[j], 16 * (layer + 1) * (S_EXP // HOUT))
            for j in range(BODY):
                sp.dma_start(hring[:, j, :], h_dram[j, :, :]).then_inc(h_loaded[j], 16)
            for n in range(RING, 2 * BODY):
                piece(v_in, row0 + n, v0 + n, n % RING)

            def v_trip(i):
                for j in range(BODY):
                    sp.wait_ge(act_ready, i * BODY + (layer * S_EXP + j - BODY + 1))
                    sp.dma_start(hring[:, j, :], h_dram[i * BODY + j, :, :]).then_inc(h_loaded[j], 16)
                    for n in (2 * j, 2 * j + 1):
                        piece(v_in, i * (2 * BODY) + (row0 + n), i * (2 * BODY) + (v0 + n), n % RING)

            with sp.Fori(1, S_EXP // BODY) as i:
                v_trip(i)

        experts(0, P_U0, P_V0)
        for j in range(RING):
            piece(w_in, P_INB - 4 * S_EXP + j, P_INB + j, j)
        sp.wait_ge(x_ready, QX * 4)
        sp.dma_start(rcon[:, :, :], dram["rcon"]).then_inc(l1_in, 16)
        sp.dma_start(posi, dram["pos"].partition_broadcast(P)).then_inc(l1_in, 16)
        sp.wait_ge(spill_done, 32)
        sp.dma_start(kvt[:, 0:4, :], spill[:, 0:1024]).then_inc(l1_in, 16)
        sp.dma_start(vn[:, :, :], spill[:, 1024:2048]).then_inc(l1_in, 16)
        stream(w_in, P_INB - 4 * S_EXP + RING, P_INB + RING, 2 * (S_INB + S_OUT + S_WQ) - RING)
        experts(1, P_U1, P_V1)
        for q in range(QX):
            sp.wait_ge(xta_ready, 3 * 8 + 2 * (q + 1))
            sp.wait_ge(xtd_ready, 3 * 8 + 2 * (q + 1))
            sp.dma_start(dram["out"][:, q * CQ:(q + 1) * CQ, :], xt[:, q * CQ:(q + 1) * CQ, :]).then_inc(out_done, 16)
        sp.wait_ge(out_done, 16 * QX)

    @block.scalar
    def _(act):
        own = Chain(act, act_own)

        def hi(p, j, first=False):
            if first:
                act.wait_ge(raw_full[j], 16)
            else:
                act.wait_ge(piece_used, p - (RING - 1))
                act.wait_ge(raw_full[j], raw_count(p, j))
            nc.scalar.activation(wh[:, j, :], raw[:, j, :], ACT.Copy).then_inc(hi_ready, 1)

        def raw_count(p, j):
            return (p - j) * (16 // RING) + 16

        def ahead(p0):
            for n in range(AHEAD):
                hi(p0 + n, n)

        def t_stage(p0, t0, n, evac, lead_first=False, done=0):
            def two(i, first):
                for s in range(2):
                    for e in range(2):
                        j = 2 * s + e
                        if not first or j >= done:
                            hi(i * RING + (p0 + j), j, first=lead_first and first)
                    if not (first and s == 0):
                        k = i * 2 + (s - 1)
                        act.wait_ge(piece_used, k * 2 + (p0 + 2))
                        evac(k, (s + 1) % 2)

            two(0, True)
            if n > 2:
                with act.Fori(1, n // 2) as i:
                    two(i, False)
            act.wait_ge(piece_used, p0 + 2 * n)
            evac(n - 1, 1)

        def copy_out(dst):
            def evac(k, bank):
                nc.scalar.activation(dst(k), ps[:, bank, 0:TOK], ACT.Copy).then_inc(evac_done, 1)
            return evac

        def n_stage(p0, s0, n, source, ready):
            with act.Fori(0, n // 2) as i:
                for s in range(2):
                    for e in range(2):
                        hi(i * RING + (p0 + 2 * s + e), 2 * s + e)
                    ready(i, s)
                    nc.scalar.activation(act_h[:, s, :], source(i, s), ACT.Copy).then_inc(acth_ready, 1)

        def split_input(n):
            for q in range(QX):
                act.wait_ge(memx_in[q], 16 * (n + 1))
                nc.scalar.activation(xh[:, q * CQ:(q + 1) * CQ, :], in_raw[:, q * CQ:(q + 1) * CQ, :],
                                     ACT.Copy).then_inc(xh_ready, 1)

        def attention(layer):
            n0 = ATT0[layer]

            def exps(g, swa):
                s = (n0 + g) % 3
                act.wait_ge(negm_ready, n0 + g + 1)
                for u in range(4):
                    last = nc.scalar.activation(ssb[:, s, u, :], ssb[:, s, u, :], ACT.Exp,
                                                bias=asm[:, s, 1, u:u + 1], accum_out=asm[:, s, 2, u:u + 1])
                    if u < 3 or swa:
                        own.mark(last)
                    else:
                        last.then_inc(p_ready, 1)
                if swa:
                    nc.scalar.activation(asm[:, s, 3, :], asm[:, s, 4, :], ACT.Exp).then_inc(p_ready, 1)

            groups = ATT[layer]
            for i in range(len(groups) + 3):
                if i < len(groups):
                    exps(i, groups[i][0])
                if 0 <= i - 2 < len(groups):
                    g = n0 + i - 2
                    act.wait_ge(pt_ready, g + 1)
                    if i - 2 >= 2:
                        act.wait_ge(o_ready, g - 1)
                    nc.scalar.activation(pt[:, g % 2, :, :, :], ps[:, 4:6, :].rearrange("p a (b c) -> p a b c", b=2),
                                         ACT.Copy).then_inc(pt_evac, 1)
                if 0 <= i - 3 < len(groups):
                    g = n0 + i - 3
                    swa, c = groups[i - 3]
                    act.wait_ge(o_ready, g + 1)
                    if swa:
                        nc.scalar.activation(cat[:, c, :], ps[:, 6 + g % 2, 0:TOK], ACT.Copy,
                                             scale=1.0 / ALPHA).then_inc(o_evac, 1)
                    else:
                        nc.scalar.activation(cat[:, MC + 2 * c:MC + 2 * c + 2, :],
                                             ps[:, 6 + g % 2, :].rearrange("p (a b) -> p a b", a=2),
                                             ACT.Copy, scale=1.0 / ALPHA).then_inc(o_evac, 1)

        def norm(n, p_next):
            if n < 3:
                ahead(p_next)
            act.wait_ge(var_ready, n + 1)
            nc.scalar.activation(lnmv[:, :, 2:3], lnmv[:, :, 1:2], ACT.Sqrt, bias=epsc,
                                 scale=ALPHA * ALPHA).then_inc(std_ready, 1)
            act.wait_ge(rstd_ready, n + 1)
            for b in (0, 2):
                nc.scalar.activation(xn[:, 0, b * 512:(b + 2) * 512], ps[:, b:b + 2, :].rearrange("p a b -> p (a b)"),
                                     ACT.Identity, bias=lnmv[:, 0, 4:5], scale=lnmv[:, 0, 3:4]).then_inc(xn0_ready, 1)
            for q in range(QX):
                b = 2 * q
                act.wait_ge(xtr_ready, 8 * n + b + 1)
                for c in (2 * b, 2 * b + 1):
                    gain, shift = C_LN + 2 * n * KC + c, C_LN + (2 * n + 1) * KC + c
                    nc.scalar.activation(xt[:, c, :], ps[:, b, (c % 2) * TOK:(c % 2 + 1) * TOK], ACT.Identity,
                                         bias=par[:, shift:shift + 1], scale=par[:, gain:gain + 1])\
                        .then_inc(xta_ready, 1)
                if n < 3:
                    act.wait_ge(xta_ready, 8 * n + 2 * (q + 1))
                    act.wait_ge(xtd_ready, 8 * n + 2 * (q + 1))
                    nc.scalar.activation(xh[:, q * CQ:(q + 1) * CQ, :], xt[:, q * CQ:(q + 1) * CQ, :],
                                         ACT.Copy).then_inc(xh_ready, 1)

        def experts(layer, u0, v0, t0):
            def gelu(k, j):
                j %= 2
                act.wait_ge(piece_used, k * 2 + (u0 + 2))
                stores = (k - j) * (16 // HOUT) + layer * 16 * (S_EXP // HOUT)
                if not (isinstance(k, int) and stores == 0):
                    act.wait_ge(h_stored[j], stores)
                nc.scalar.activation(hring[:, j, :], ps[:, j, 0:TOK], ACT.Gelu).then_inc(evac_done, 1)

            def gates_out(q, k):
                act.wait_ge(g_ready, q + (layer * TOK // 4 + 1))
                nc.scalar.activation(gate_of[:, :, bass.ds(q * 4, 4)].rearrange("p i t -> p t i"),
                                     ps[:, 2 + k % 4, :].rearrange("p (t i) -> p t i", t=4),
                                     ACT.Copy).then_inc(g_evac, 1)

            def trip(i, slabs, first, spread, spread_first=False):
                for s in range(slabs):
                    for n in (2 * s, 2 * s + 1):
                        hi(i * (2 * slabs) + (u0 + n), n % RING)
                    if not (first and s == 0):
                        gelu(i * slabs + (s - 1), s - 1)
                    if spread and not (spread_first and s == 0):
                        for k in (2 * s - 2, 2 * s - 1):
                            gates_out((i - SPREAD0) * Q_TRIP + k, k)

            trip(0, ROUTE, True, False)
            with act.Fori(1, UNITS) as i:
                trip(i, ROUTE, False, False)
            act.wait_ge(gd_ready, layer + 1)
            nc.scalar.activation(sel[:, 2, :], sel[:, 2, :], ACT.Exp).then_inc(ge_ready, 1)
            for w in range(3):
                act.wait_ge(selt_ready, layer * 3 + w + 1)
                nc.scalar.activation(sel_t[:, w, :], ps[:, 2 + w, 0:TOK], ACT.Copy).then_inc(selt_evac, 1)
            trip(SPREAD0, BODY, False, True, True)
            with act.Fori(SPREAD0 + 1, TRIPS_E) as i:
                trip(i, BODY, False, True)
            gelu(S_EXP - 1, S_EXP - 1)
            for k in (2, 1):
                gates_out(TOK // 4 - k, -k)

            def ready(i, s):
                act.wait_ge(act_ready, i * 2 + (layer * S_EXP + s + 1))
            n_stage(v0, layer * S_EXP, S_EXP, lambda i, s: act_t[:, s, :], ready)

        split_input(0)
        t_stage(P_MEM, T_MEM, S_MEM, copy_out(lambda k: kvt_all[:, k, :]), lead_first=True)
        act.wait_ge(l0_in, 32)
        nc.scalar.activation(dtw_r[:, 0:KC, 0, :], dtw[:, :, :], ACT.Copy).then_inc(dtwh_ready, 1)
        nc.scalar.activation(dtw_r[:, KC:KC + 2, 0, :], dtw[:, 0:2, :], ACT.Copy).then_inc(dtwh_ready, 1)
        nc.scalar.activation(dtw_r[:, KC:KC + 2, 1, :], dtw[:, 0:2, :], ACT.Copy).then_inc(dtwh_ready, 1)
        for n in range(4):
            act.wait_ge(vtr_ready, n + 1)
            dst = vn[:, n, :] if n < 2 else vn_spill[:, n - 2, :]
            nc.scalar.activation(dst, ps[:, 2 + n, :], ACT.Copy).then_inc(vn_ready, 1)
        nc.scalar.activation(kvt[:, 0:4, :], kvt_all[:, 0:4, :], ACT.Copy).then_inc(vn_ready, 1)
        act.wait_ge(piece_used, P_MEM + 2 * S_MEM)
        split_input(1)
        act.wait_ge(spill_done, 32)
        act.wait_ge(vn_ready, 5)
        t_stage(P_INA, T_INA, S_INA, copy_out(lambda k: proj[:, k, LPAD:LPAD + TOK]))

        act.wait_ge(dtx_ready, 1)
        own.mark(nc.scalar.activation(dts[:, 2, :], dts[:, 1, :], ACT.Exp, scale=-1.0))
        nc.scalar.activation(dts[:, 4, 0:24], par[:, R_ALOG:R_ALOG + 24], ACT.Exp).then_inc(dte_ready, 1)
        own.sync()
        nc.scalar.activation(dts[:, 3, :], dts[:, 2, :], ACT.Ln, bias=1.0).then_inc(dtl_ready, 1)
        act.wait_ge(conv_done, 1)
        nc.scalar.activation(xc[:, MC:XBC_C, :], xc[:, MC:XBC_C, :], ACT.Silu).then_inc(silu_done, 1)
        nc.scalar.activation(xc[:, 0:MC, :], xc[:, 0:MC, :], ACT.Silu).then_inc(silu_done, 1)
        act.wait_ge(adt_ready, 1)
        nc.scalar.activation(adt_r[:, 0, :], dts[:, 6, :], ACT.Copy).then_inc(adth_ready, 1)
        for g in range(GROUPS):
            act.wait_ge(cb_ready, g + 1)
            nc.scalar.activation(cbm[:, g, P:2 * P], ps[:, 2 + g, P:2 * P], ACT.Copy).then_inc(cbo_ready, 1)
        act.wait_ge(evac_done, T_INA + S_INA)
        nc.scalar.activation(proj[:, XBC_C:XBC_C + MC, LPAD:LPAD + TOK],
                             proj[:, XBC_C:XBC_C + MC, LPAD:LPAD + TOK], ACT.Silu).then_inc(silu_done, 1)
        act.wait_ge(cs_evac, 1)
        for h in range(SSM_HEADS):
            s = h % 2
            act.wait_ge(row_ready, h + 1)
            if h >= 2:
                act.wait_ge(m_ready, h - 1)
            bias = (dts[:, 7, h:h + 1], dts[:, 8, h:h + 1], dts[:, 7, 24 + h:25 + h])
            for b in range(3):
                ins = nc.scalar.activation(ex[:, s, b * P:(b + 1) * P], ps[:, 6 + s, b * P:(b + 1) * P], ACT.Exp,
                                           bias=bias[b])
                if b < 2:
                    own.mark(ins)
                else:
                    ins.then_inc(ex_ready, 1)
        for g in range(GROUPS):
            act.wait_ge(y_done, MC)
            if g >= 2:
                act.wait_ge(ms_ready, g - 1)
            nc.scalar.activation(ysq[:, g % 2, :, :], cat[:, g * GC:(g + 1) * GC, :], ACT.Square).then_inc(ysq_ready, 1)
            act.wait_ge(ms_ready, g + 1)
            if g == 0:
                act.wait_ge(eps_set, 1)
            nc.scalar.activation(nrm[:, g, :], ps[:, 2 + g % 2, 0:TOK], ACT.Sqrt, bias=epsc).then_inc(rms_ready, 1)
        attention(0)
        act.wait_ge(cat_ready, 1)
        act.wait_ge(o_evac, 2)
        n_stage(P_OUT0, 0, S_OUT, lambda i, s: cat[:, i * 2 + s, :], lambda i, s: None)
        norm(0, P_WQ0)
        t_stage(P_WQ0, T_WQ0, S_WQ, copy_out(lambda k: qt[:, k, :]), done=AHEAD)
        experts(0, P_U0, P_V0, T_U0)
        norm(1, P_INB)

        t_stage(P_INB, T_INB, S_INB, copy_out(lambda k: proj1[:, k, :]), done=AHEAD)
        act.wait_ge(trig_in, 1)
        nc.scalar.activation(cs[:, :, :], ang[:, 0:2, :], ACT.Sin).then_inc(cossin_ready, 1)
        for k in range(KV_HEADS):
            act.wait_ge(kdup_ready, k + 1)
            nc.scalar.activation(kdup[:, k, :], ps[:, 2 + k, 0:TOK], ACT.Copy).then_inc(kdup_evac, 1)
        act.wait_ge(vtr1_ready, 1)
        nc.scalar.activation(vn1[:, :, :], ps[:, 6, :].rearrange("p (a b) -> p a b", a=2), ACT.Copy).then_inc(vn1_ready, 1)
        attention(1)
        act.wait_ge(o_evac, 16)
        n_stage(P_OUT1, 0, S_OUT, lambda i, s: cat[:, i * 2 + s, :], lambda i, s: None)
        norm(2, P_WQ1)
        t_stage(P_WQ1, T_WQ1, S_WQ, copy_out(lambda k: qt[:, k, :]), done=AHEAD)
        experts(1, P_U1, P_V1, T_U1)
        norm(3, None)

    @block.tensor
    def _(pe):
        def mm(out, lhs, rhs, start, stop, **kw):
            return nc.tensor.matmul(out, lhs, rhs, start=start, stop=stop, **kw)

        def slab_t(piece, slab, par_, s4, first=False, x_from=None, then=None):
            if not first:
                pe.wait_ge(evac_done, slab - 1)
            out = ps[:, par_, 0:TOK]
            for e in range(2):
                j = (2 * s4 + e) % RING
                pe.wait_ge(lo_ready, piece + (e + 1))
                for k in range(KC // 2):
                    kc = e * (KC // 2) + k
                    if x_from is not None and kc % CQ == 0:
                        pe.wait_ge(x_ready, x_from + kc // CQ + 1)
                    w_hi, w_lo = (w[:, j, k * P:(k + 1) * P] for w in (wh, wl))
                    mm(out, w_hi, xh[:, kc, :], kc == 0, False)
                    mm(out, w_hi, xl[:, kc, :], False, False)
                    last = mm(out, w_lo, xh[:, kc, :], False, kc == KC - 1)
                last.then_inc(piece_used, 1)
                if then is not None:
                    then(e)

        def t_stage(p0, t0, n, x_count):
            lead = t0 == 0
            for s in range(2):
                slab_t(p0 + 2 * s, t0 + s, s, s, first=lead, x_from=QX * (x_count - 1) if s == 0 else None)
            with pe.Fori(1, n // 2) as i:
                for s in range(2):
                    slab_t(i * RING + (p0 + 2 * s), i * 2 + (t0 + s), s, s)

        def slab_n(piece, chunk, s):
            pe.wait_ge(actl_ready, chunk + 1)
            for e in range(2):
                j = 2 * s + e
                pe.wait_ge(lo_ready, piece + (e + 1))
                for t in range(NT):
                    a_h, a_l = (a[:, s, t * P:(t + 1) * P] for a in (act_h, act_l))
                    for q in range(2):
                        out = ps[:, 4 * t + 2 * e + q, :]
                        w_hi, w_lo = (w[:, j, q * 512:(q + 1) * 512] for w in (wh, wl))
                        mm(out, a_h, w_hi, False, False, skip_group_check=True)
                        mm(out, a_h, w_lo, False, False, skip_group_check=True)
                    for q in range(2):
                        last = mm(ps[:, 4 * t + 2 * e + q, :], a_l, wh[:, j, q * 512:(q + 1) * 512], False, False,
                                  skip_group_check=True)
                last.then_inc(piece_used, 1)

        def n_stage(k, p0, c0, n):
            if k == 0:
                pe.wait_ge(ident_ready, 1)
            for t in range(NT):
                for c in range(KC):
                    out = ps[:, 4 * t + c // 4, (c % 4) * P:(c % 4 + 1) * P]
                    x_h, x_l = (x[:, c, t * P:(t + 1) * P] for x in (xh, xl))
                    mm(out, x_h, ident_r, c % 4 == 0, False, skip_group_check=True)
                    mm(out, x_l, ident_r, False, False, skip_group_check=True)
            with pe.Fori(0, n // 2) as i:
                for s in range(2):
                    slab_n(i * RING + (p0 + 2 * s), i * 2 + (c0 + s), s)

        def to_dims(n):
            pe.wait_ge(xn0_ready, 2 * n + 1)
            pe.wait_ge(xn1_ready, 2 * n + 1)
            for b in range(8):
                if b == 2:
                    pe.wait_ge(xn0_ready, 2 * n + 2)
                if b == 4:
                    pe.wait_ge(xn1_ready, 2 * n + 2)
                for c in range(2):
                    for t in range(NT):
                        last = nc.tensor.transpose(ps[:, b, c * TOK + t * P:c * TOK + (t + 1) * P],
                                                   xn[:, t, (2 * b + c) * P:(2 * b + c + 1) * P], ident)
                last.then_inc(xtr_ready, 1)

        def attention(layer):
            n0, groups = ATT0[layer], ATT[layer]

            def scores(g):
                swa, c = groups[g]
                s = (n0 + g) % 2
                if g >= 2:
                    pe.wait_ge(negm_ready, n0 + g - 1)
                for r in range(2):
                    for t in range(NT):
                        out = ps[:, 2 * s + r, t * TOK:(t + 1) * TOK]
                        if swa:
                            rows = slice(64 * r, 64 * r + 64)
                            last = mm(out, proj1[rows, 4 + c, t * P:(t + 1) * P],
                                      kdup[rows, 2 * c // (ATT_HEADS // KV_HEADS), :], True, True)
                        else:
                            h = 2 * c + r
                            q = proj1[:, 16 + h, :] if layer else proj[:, XBC_C + MC + h, LPAD:LPAD + TOK]
                            last = mm(out, q[:, t * P:(t + 1) * P], kvt[:, h, :], True, True)
                last.then_inc(s_ready, 1)

            for i in range(len(groups) + 3):
                if i < len(groups):
                    scores(i)
                if 0 <= i - 2 < len(groups):
                    g = n0 + i - 2
                    pe.wait_ge(pn_ready, g + 1)
                    if i - 2 >= 1:
                        pe.wait_ge(pt_evac, g)
                    for r in range(2):
                        for t in range(NT):
                            for k in range(2):
                                last = nc.tensor.transpose(ps[:, 4 + r, k * TOK + t * P:k * TOK + (t + 1) * P],
                                                           ssb[:, g % 3, 2 * r + t, k * P:(k + 1) * P], ident)
                    last.then_inc(pt_ready, 1)
                if 0 <= i - 3 < len(groups):
                    g = n0 + i - 3
                    swa, c = groups[i - 3]
                    pe.wait_ge(pt_evac, g + 1)
                    if i - 3 >= 2:
                        pe.wait_ge(o_evac, g - 1)
                    for r in range(2):
                        for k in range(2):
                            if swa:
                                kv = 2 * c // (ATT_HEADS // KV_HEADS)
                                last = mm(ps[64 * r:64 * r + 64, 6 + g % 2, 0:TOK], vn1[:, k, kv * 64:kv * 64 + 64],
                                          pt[:, g % 2, r, k, :], k == 0, k == 1)
                            else:
                                h = 2 * c + r
                                last = mm(ps[:, 6 + g % 2, r * TOK:(r + 1) * TOK], vn[:, k, h * P:(h + 1) * P],
                                          pt[:, g % 2, r, k, :], k == 0, k == 1)
                    last.then_inc(o_ready, 1)

        def experts(layer, u0, v0, t0):
            pe.wait_ge(subk_in, 16 * (layer + 1))
            pe.wait_ge(evac_done, t0)
            for b in range(UNITS // 4):
                if b == 3:
                    pe.wait_ge(sc_evac, 4 * layer + 1)
                for u4 in range(4):
                    u = 4 * b + u4
                    t, h = u // PEER_H, u % PEER_H
                    for half in range(2):
                        rows = slice(64 * half, 64 * half + 64)
                        last = mm(ps[:, 2 + 2 * (b % 3) + half, u4 * P:(u4 + 1) * P],
                                  qt[rows, h, t * P:(t + 1) * P], subk[rows, h, :], True, True)
                last.then_inc(sc_ready, 1)

            def spread(q, k):
                pe.wait_ge(hot_ready, q + (layer * TOK // 4 + 1))
                if not isinstance(q, int) or layer or q >= 4:
                    pe.wait_ge(g_evac, q + (layer * TOK // 4 - 3))
                for t in range(4):
                    last = mm(ps[:, 2 + k % 4, t * P:(t + 1) * P], hot[:, k % 2, 0, t, :], hot[:, k % 2, 1, t, :],
                              True, True)
                last.then_inc(g_ready, 1)

            def trip(i, slabs, spreads):
                for s in range(slabs):
                    then = None
                    if spreads:
                        def then(e, s=s):
                            spread((i - SPREAD0) * Q_TRIP + (2 * s + e), 2 * s + e)
                    slab_t(i * (2 * slabs) + (u0 + 2 * s), i * slabs + (t0 + s), s % 2, s, then=then)

            with pe.Fori(0, UNITS) as i:
                trip(i, ROUTE, False)
            for w in range(3):
                pe.wait_ge(sel_ready, layer + 1)
                for t in range(NT):
                    last = nc.tensor.transpose(ps[:, 2 + w, t * P:(t + 1) * P], sel[:, w, t * P:(t + 1) * P], ident)
                last.then_inc(selt_ready, 1)
            trip(SPREAD0, BODY, True)
            with pe.Fori(SPREAD0 + 1, TRIPS_E) as i:
                trip(i, BODY, True)
            pe.wait_ge(evac_done, t0 + S_EXP)
            pe.wait_ge(g_evac, (layer + 1) * TOK // 4)
            n_stage(2 * layer + 1, v0, (layer + 1) * S_OUT + layer * S_EXP, S_EXP)

        pe.wait_ge(consts_in, 48)
        t_stage(P_MEM, T_MEM, S_MEM, 1)
        pe.wait_ge(evac_done, T_MEM + S_MEM)
        for n in range(4):
            for h in range(MEM_HEADS):
                last = nc.tensor.transpose(ps[:, 2 + n, h * P:(h + 1) * P],
                                           kvt_all[:, 8 * (n // 2) + 4 + h, (n % 2) * P:(n % 2 + 1) * P], ident)
            last.then_inc(vtr_ready, 1)
        pe.wait_ge(dtw_ready, 1)
        for c in range(KC):
            if c % CQ == 0:
                pe.wait_ge(x_ready, QX + c // CQ + 1)
            w = dtw_f[:, c * 2 * SSM_HEADS:c * 2 * SSM_HEADS + P]
            mm(ps[:, 6, 0:TOK], w, xh[:, c, :], c == 0, False)
            last = mm(ps[:, 6, 0:TOK], w, xl[:, c, :], False, c == KC - 1)
        last.then_inc(dtc_ready, 1)
        t_stage(P_INA, T_INA, XBC_C, 2)
        pe.wait_ge(dtc_evac, 1)
        for t in range(NT):
            last = nc.tensor.transpose(ps[:, 7, t * P:(t + 1) * P], dt_c[:, t * P:(t + 1) * P], ident)
        last.then_inc(dt_ready, 1)
        t_stage(P_INA + 2 * XBC_C, T_INA + XBC_C, S_INA - XBC_C, 2)

        tri, strict = lcon[:, 0, :], lcon[:, 1, :]
        pe.wait_ge(adt_ready, 1)
        mm(ps[:, 6, 0:48], tri, dts[:, 6, :], True, True)
        mm(ps[:, 6, 64:88], strict, dts[:, 6, 0:24], True, True).then_inc(cs_ready, 1)
        pe.wait_ge(silu_done, 1)
        for g in range(GROUPS):
            b_t, c_t = xc[:, MC + g, :], xc[:, MC + GROUPS + g, :]
            mm(ps[:, 2 + g, 0:TOK], b_t[:, 0:P], c_t, True, True)
            mm(ps[:, 2 + g, TOK:TOK + P], b_t[:, P:TOK], c_t[:, P:TOK], True, True).then_inc(cb_ready, 1)
        pe.wait_ge(silu_done, 2)
        pe.wait_ge(evac_done, T_INA + S_INA)
        for b in range(6):
            if b >= 2:
                pe.wait_ge(cbm_ready, b - 1)
                pe.wait_ge(cbo_ready, b - 1)
            for c in range(2):
                for t in range(NT):
                    last = nc.tensor.transpose(ps[:, b, c * TOK + t * P:c * TOK + (t + 1) * P],
                                               xc[:, 2 * b + c, t * P:(t + 1) * P], ident)
            last.then_inc(xst_ready, 1)
        pe.wait_ge(cs_evac, 1)
        pe.wait_ge(adtr_ready, 1)

        def rows(h):
            if h >= 2:
                pe.wait_ge(ex_ready, h - 1)
            bank = ps[:, 6 + h % 2, :]
            for k in range(2):
                a0, a1 = (adt_r[:, k, t * 24 + h:t * 24 + h + 1].broadcast_to([P, P]) for t in range(NT))
                mm(bank[:, 0:P], a0, tri_r[:, 0, :], k == 0, False, skip_group_check=True)
                mm(bank[:, P:3 * P], a1, tri_r[:, :, :], False, False, skip_group_check=True)
            mm(bank[:, 0:P], ident_b, later_b, False, False, skip_group_check=True)
            mm(bank[:, 2 * P:3 * P], ident_b, later_b, False, True, skip_group_check=True).then_inc(row_ready, 1)

        rows(0)
        for h in range(SSM_HEADS):
            if h + 1 < SSM_HEADS:
                rows(h + 1)
            c, r, s = h // 2, h % 2, h % 2
            if h == 0:
                pe.wait_ge(xdt_ready, 6)
            pe.wait_ge(m_ready, h + 1)
            if c >= 2 and r == 0:
                pe.wait_ge(y_done, c - 1)
            mm(ps[64 * r:64 * r + 64, c % 2, 0:TOK], xdt[:, 0, h, :], mt[:, s, 0:TOK], True, False)
            mm(ps[64 * r:64 * r + 64, c % 2, P:TOK], xdt[:, 1, h, :], mt[:, s, TOK:TOK + P], False, True)\
                .then_inc(y_ready, 1)
        for g in range(GROUPS):
            pe.wait_ge(ysq_ready, g + 1)
            if g >= 2:
                pe.wait_ge(rms_ready, g - 1)
            for c in range(GC):
                last = mm(ps[:, 2 + g % 2, 0:TOK], lcon[:, 2, :], ysq[:, g % 2, c, :], c == 0, c == GC - 1)
            last.then_inc(ms_ready, 1)
        pe.wait_ge(y_done, MC)
        pe.wait_ge(rms_ready, GROUPS)
        attention(0)
        pe.wait_ge(o_evac, 2)
        n_stage(0, P_OUT0, 0, S_OUT)
        to_dims(0)
        t_stage(P_WQ0, T_WQ0, S_WQ, 3)
        experts(0, P_U0, P_V0, T_U0)
        to_dims(1)

        t_stage(P_INB, T_INB, S_INB, 4)
        pe.wait_ge(l1_in, 64)
        pe.wait_ge(evac_done, T_INB + S_INB)
        for n in range(14):
            c = n if n < 2 else n + 2
            if n >= 2:
                pe.wait_ge(rope_done, n - 1)
            mm(ps[:, n % 2, 0:TOK], rcon[:, 0, :], proj1[:, c, :], True, True).then_inc(rot_ready, 1)
        for k in range(KV_HEADS):
            pe.wait_ge(rope_done, 2)
            mm(ps[:, 2 + k, 0:TOK], rcon[:, 1 + k % 2, :], proj1[:, k // 2, :], True, True).then_inc(kdup_ready, 1)
        for t in range(NT):
            for c in range(2):
                last = nc.tensor.transpose(ps[:, 6, t * TOK + c * P:t * TOK + (c + 1) * P],
                                           proj1[:, 2 + c, t * P:(t + 1) * P], ident)
        last.then_inc(vtr1_ready, 1)
        pe.wait_ge(rope_done, 14)
        pe.wait_ge(kdup_evac, KV_HEADS)
        pe.wait_ge(vn1_ready, 1)
        attention(1)
        pe.wait_ge(o_evac, 16)
        n_stage(2, P_OUT1, S_OUT + S_EXP, S_OUT)
        to_dims(2)
        t_stage(P_WQ1, T_WQ1, S_WQ, 5)
        experts(1, P_U1, P_V1, T_U1)
        to_dims(3)

    @block.vector
    def _(dve):
        own = Chain(dve, dve_own, dve_settled)
        v = nc.vector

        def lo(p, j):
            dve.wait_ge(hi_ready, p + 1)
            v.tensor_tensor(wl[:, j, :], raw[:, j, :], wh[:, j, :].bitcast(F32), ALU.subtract).then_inc(lo_ready, 1)

        def ahead(p0):
            for n in range(AHEAD):
                lo(p0 + n, n)

        def split_t(p0, n, done=0):
            if done:
                for j in range(done, RING):
                    lo(p0 + j, j)
            with dve.Fori(1 if done else 0, 2 * n // RING) as i:
                for j in range(RING):
                    lo(i * RING + (p0 + j), j)

        def low_x(src, n):
            for q in range(QX):
                low_quarter(src, n, q)

        def low_quarter(src, n, q):
            part = slice(q * CQ, (q + 1) * CQ)
            dve.wait_ge(xh_ready, QX * n + q + 1)
            v.tensor_tensor(xl[:, part, :], src[:, part, :], xh[:, part, :].bitcast(F32), ALU.subtract)\
                .then_inc(x_ready, 1)

        def act_low(src, chunk, s):
            dve.wait_ge(acth_ready, chunk + 1)
            v.tensor_tensor(act_l[:, s, :], src, act_h[:, s, :].bitcast(F32), ALU.subtract).then_inc(actl_ready, 1)

        def split_n(p0, c0, n, source):
            with dve.Fori(0, n // 2) as i:
                for s in range(2):
                    for e in range(2):
                        lo(i * RING + (p0 + 2 * s + e), 2 * s + e)
                    act_low(source(i, s), i * 2 + (c0 + s), s)

        def attention(layer):
            n0, groups = ATT0[layer], ATT[layer]

            def top(g):
                swa, c = groups[g]
                s, bank = (n0 + g) % 3, 2 * ((n0 + g) % 2)
                dve.wait_ge(s_ready, n0 + g + 1)
                if g >= 3:
                    dve.wait_ge(pt_ready, n0 + g - 2)
                banks = ps[:, bank:bank + 2, :]
                flat = ssb[:, s, :, :].rearrange("p (a b) c -> p a (b c)", a=2)
                mx, negm, es, sd = (asm[:, s, k, :] for k in (0, 1, 3, 4))
                if swa:
                    mask = rcon[:, 3:7, :].rearrange("p a b -> p (a b)").unsqueeze(1).broadcast_to([P, 2, 2 * TOK])
                    own.link(v.scalar_tensor_tensor(out=flat, in0=banks, scalar=64 ** -0.5, in1=mask,
                                                    op0=ALU.mult, op1=ALU.add))
                else:
                    own.link(v.tensor_scalar(flat, banks, MEM_D ** -0.5, None, ALU.mult))
                own.link(v.tensor_reduce(mx, ssb[:, s, :, :], AX.X, ALU.max))
                if swa:
                    sink = par[:, R_SINK + 2 * c:R_SINK + 2 * c + 2].unsqueeze(2).broadcast_to([P, 2, 2])
                    mx2, sd2 = (m.rearrange("p (a b) -> p a b", a=2) for m in (mx, sd))
                    own.link(v.tensor_tensor(mx2, mx2, sink, ALU.max))
                    own.mark(v.tensor_tensor(sd2, sink, mx2, ALU.subtract))
                    own.sync()
                v.tensor_scalar(negm, mx, -1.0, None, ALU.mult).then_inc(negm_ready, 1)

            def normalise(g):
                swa, c = groups[g]
                s = (n0 + g) % 3
                den, es = asm[:, s, 2, :], asm[:, s, 3, :]
                dve.wait_ge(p_ready, n0 + g + 1)
                dve.wait_ge(act_own, att_own(layer, g))
                if swa:
                    own.link(v.tensor_tensor(den, den, es, ALU.add))
                own.link(v.reciprocal(den, den))
                v.tensor_tensor(ssb[:, s, :, :], ssb[:, s, :, :], den.unsqueeze(2).broadcast_to([P, 4, TOK]),
                                ALU.mult).then_inc(pn_ready, 1)

            top(0)
            for g in range(len(groups)):
                if g + 1 < len(groups):
                    top(g + 1)
                normalise(g)

        def att_own(layer, g):
            n = 1 + 2 * SSM_HEADS
            for l, groups in enumerate(ATT):
                for k, (swa, _) in enumerate(groups):
                    n += 4 if swa else 3
                    if (l, k) == (layer, g):
                        return n

        def norm(n, p_end, p_next):
            if n < 3:
                lo(p_next, 0)
                lo(p_next + 1, 1)
            for half in range(2):
                dve.wait_ge(piece_used, p_end - 1 + half)
                for t in range(NT):
                    for q in (2 * half, 2 * half + 1):
                        own.mark(v.bn_stats(out=lnst[:, t, q, :], in_=ps[:, 4 * t + q, :]))
            own.sync()
            for t in range(NT):
                own.mark(v.bn_aggr(out=lnmv[:, t, 0:2], in_=lnst[:, t, :, :].rearrange("p a b -> p (a b)")))
            own.sync()
            v.tensor_scalar(lnmv[:, :, 5:6], lnmv[:, :, 0:1], -1.0, None, ALU.mult).then_inc(var_ready, 1)
            if n < 3:
                lo(p_next + 2, 2)
            dve.wait_ge(std_ready, n + 1)
            own.link(v.reciprocal(lnmv[:, :, 3:4], lnmv[:, :, 2:3]))
            own.link(v.tensor_scalar(lnmv[:, :, 3:4], lnmv[:, :, 3:4], ALPHA, None, ALU.mult))
            dve.wait_ge(var_ready, n + 1)
            v.tensor_tensor(lnmv[:, :, 4:5], lnmv[:, :, 5:6], lnmv[:, :, 3:4], ALU.mult).then_inc(rstd_ready, 1)
            for b in (0, 2):
                v.tensor_scalar(xn[:, 1, b * 512:(b + 2) * 512], ps[:, 4 + b:6 + b, :].rearrange("p a b -> p (a b)"),
                                lnmv[:, 1, 0:1], lnmv[:, 1, 3:4], ALU.subtract, ALU.mult).then_inc(xn1_ready, 1)
            for q in range(QX):
                b = 2 * q + 1
                dve.wait_ge(xtr_ready, 8 * n + b + 1)
                for c in (2 * b, 2 * b + 1):
                    gain, shift = C_LN + 2 * n * KC + c, C_LN + (2 * n + 1) * KC + c
                    v.tensor_scalar(xt[:, c, :], ps[:, b, (c % 2) * TOK:(c % 2 + 1) * TOK], par[:, gain:gain + 1],
                                    par[:, shift:shift + 1], ALU.mult, ALU.add).then_inc(xtd_ready, 1)
                if n < 3 and q >= 1:
                    low_quarter(xt, n + 2, q - 1)
            if n < 3:
                low_quarter(xt, n + 2, QX - 1)

        def experts(layer, u0, v0, c0):
            for b in range(UNITS // 4):
                dve.wait_ge(sc_ready, 4 * layer + b + 1)
                bank = 2 + 2 * (b % 3)
                v.tensor_copy(sc[:, 4 * b:4 * b + 4, :, :].rearrange("p u t k -> p t u k"),
                              ps[:, bank:bank + 2, :].rearrange("p t (u k) -> p t u k", u=4)).then_inc(sc_evac, 1)
            dve.wait_ge(sc_evac, 4 * layer + 4)

            s0, s1 = sw[:, 0], sw[:, 1]
            sums, left = (cand[:, k].rearrange("p a b -> p (a b)") for k in range(2))
            pairs = pick.rearrange("p (w k) a -> p w k a", w=2)

            def unit(i, head=True, tail=True):
                def low(*pieces):
                    if head:
                        for n in pieces:
                            lo(i * (2 * ROUTE) + (u0 + n), n % RING)
                    own.sync()

                if head:
                    own.mark(v.tensor_copy(s0, sc[:, i, :, :]))
                if tail:
                    own.mark(v.max_index(best_i[:, 0, 8:16], best_v[:, 8:16], left))
                low(0)
                if tail:
                    own.mark(v.tensor_scalar(best_i[:, 1, :], best_i[:, 0, :], 4, None, ALU.logical_shift_right))
                    own.mark(v.tensor_scalar(best_i[:, 2, :], best_i[:, 0, :], TOPK - 1, None, ALU.bitwise_and))
                if head:
                    for t in range(2):
                        own.mark(v.max(top_v[:, t, 0:8], s0[:, t, :]))
                low(1, 2)
                if tail:
                    own.mark(v.tensor_copy(best_f, best_i[:, 1:3, :]))
                    own.mark(v.tensor_scalar(sel[:, 2, bass.ds((i - 1) * TOPK, TOPK)], best_v, best_v[:, 0:1], None,
                                             ALU.subtract))
                if head:
                    for t in range(2):
                        own.mark(v.max_index(top_i[:, t, 0:8], top_v[:, t, 0:8], s0[:, t, :]))
                        own.mark(v.match_replace(out=s1[:, t, :], in_to_replace=top_v[:, t, 0:8],
                                                 in_values=s0[:, t, :], imm_value=NEG))
                low(3)
                if tail:
                    own.mark(v.tensor_tensor(pick, best_f.rearrange("p w k -> p (w k)").unsqueeze(2)
                                             .broadcast_to([P, 2 * TOPK, TOPK]),
                                             iota[:, 0:TOPK].unsqueeze(1).broadcast_to([P, 2 * TOPK, TOPK]),
                                             ALU.is_equal))
                if head:
                    for t in range(2):
                        own.mark(v.max(top_v[:, t, 8:16], s1[:, t, :]))
                low(4, 5)
                if tail:
                    own.mark(v.tensor_tensor(pairs, pairs, top_f.unsqueeze(2).broadcast_to([P, 2, TOPK, TOPK]),
                                             ALU.mult))
                if head:
                    own.mark(v.tensor_tensor(cand[:, 0], top_v[:, 0, :].unsqueeze(2).broadcast_to([P, TOPK, TOPK]),
                                             top_v[:, 1, :].unsqueeze(1).broadcast_to([P, TOPK, TOPK]), ALU.add))
                    for t in range(2):
                        own.mark(v.max_index(top_i[:, t, 8:16], top_v[:, t, 8:16], s1[:, t, :]))
                low(6)
                if tail:
                    own.mark(v.tensor_reduce(sel[:, 0:2, bass.ds((i - 1) * TOPK, TOPK)], pairs, AX.X, ALU.add))
                if head:
                    own.mark(v.max(best_v[:, 0:8], sums))
                low(7, 8)
                if head:
                    own.mark(v.tensor_copy(top_f, top_i))
                    own.mark(v.max_index(best_i[:, 0, 0:8], best_v[:, 0:8], sums))
                    own.mark(v.match_replace(out=left, in_to_replace=best_v[:, 0:8], in_values=sums, imm_value=NEG))
                    low(9)
                    lo(i * (2 * ROUTE) + (u0 + 10), 10 % RING)
                    lo(i * (2 * ROUTE) + (u0 + 11), 11 % RING)
                    own.mark(v.max(best_v[:, 8:16], left))
                    own.sync()

            unit(0, tail=False)
            with dve.Fori(1, UNITS) as i:
                own.enter(i, 1, 25)
                unit(i)
            own.leave(UNITS - 1)
            unit(UNITS, head=False)
            own.sync()
            v.tensor_copy(gsm[:, 0, 0:1], iota[:, 0:1]).then_inc(gd_ready, 1)
            dve.wait_ge(ge_ready, layer + 1)
            gates = sel[:, 2, :].rearrange("p (u k) -> p u k", k=TOPK)
            own.link(v.tensor_reduce(gsm[:, 0, :], gates, AX.X, ALU.add))
            own.link(v.tensor_scalar(gsm[:, 0, :], gsm[:, 0, :], ALPHA, None, ALU.mult))
            own.link(v.reciprocal(gsm[:, 1, :], gsm[:, 0, :]))
            v.tensor_tensor(gates, gates, gsm[:, 1, :].unsqueeze(2).broadcast_to([P, UNITS, TOPK]),
                            ALU.mult).then_inc(sel_ready, 1)
            dve.wait_ge(selt_evac, 3 * layer + 3)

            def spread(i):
                for k in range(Q_TRIP):
                    q = (i - SPREAD0) * Q_TRIP + k
                    lo(i * (2 * BODY) + (u0 + k), k % RING)

                    def of(w):
                        return sel_t[:, w, bass.ds(q * 4, 4)].unsqueeze(2).broadcast_to([P, 4, P])
                    rows = iota.unsqueeze(1).broadcast_to([P, 4, P])
                    if not isinstance(q, int) or layer or q >= 2:
                        dve.wait_ge(g_ready, q + (layer * TOK // 4 - 1))
                    row2, row1 = hot[:, k % 2, 0], hot[:, k % 2, 1]
                    own.mark(v.tensor_tensor(row1, rows, of(0), ALU.is_equal))
                    own.mark(v.tensor_tensor(row2, rows, of(1), ALU.is_equal))
                    own.sync()
                    v.tensor_tensor(row1, row1, of(2), ALU.mult).then_inc(hot_ready, 1)

            spread(SPREAD0)
            with dve.Fori(SPREAD0 + 1, TRIPS_E) as i:
                own.enter(i, SPREAD0 + 1, 2 * Q_TRIP)
                spread(i)
            own.leave(TRIPS_E - SPREAD0 - 1)
            dve.wait_ge(g_evac, (layer + 1) * TOK // 4)
            with dve.Fori(0, S_EXP // BODY) as i:
                for k in range(BODY):
                    s = k % 2
                    n = i * BODY + (layer * S_EXP + k)
                    dve.wait_ge(h_loaded[k], i * 16 + 16 * (layer * (S_EXP // BODY) + 1))
                    dve.wait_ge(actl_ready, i * BODY + (c0 + k - 1))
                    v.tensor_tensor(act_t[:, s, :], hring[:, k, :], gate_of[:, i * BODY + k, :],
                                    ALU.mult).then_inc(act_ready, 1)
                    for e in range(2):
                        lo(i * (2 * BODY) + (v0 + 2 * k + e), (2 * k + e) % RING)
                    dve.wait_ge(act_ready, n + 1)
                    act_low(act_t[:, s, :], i * BODY + (c0 + k), s)

        v.memset(epsc, EPS).then_inc(eps_set, 1)
        low_x(in_raw, 0)
        split_t(P_MEM, S_MEM)
        dve.wait_ge(dtwh_ready, 3)
        v.tensor_tensor(dtw_r[:, 0:KC, 1, :], dtw[:, :, :], dtw_r[:, 0:KC, 0, :].bitcast(F32), ALU.subtract).then_inc(dtw_ready, 1)
        low_x(in_raw, 1)
        own.mark(v.memset(lcon[:, 2, :], 1.0 / (GC * P)))
        dve.wait_ge(spill_done, 32)
        dve.wait_ge(vn_ready, 5)
        own.mark(v.memset(proj[:, 0:XBC_C, 0:LPAD], 0.0))
        dve.wait_ge(consts_in, 48)
        dve.wait_ge(l0_in, 32)
        own.mark(v.tensor_copy(ident_b, ident))
        own.mark(v.tensor_scalar(par[:, C_NORMG:C_NORMG + MC], par[:, C_NORMG:C_NORMG + MC], 1.0 / ALPHA, None, ALU.mult))
        v.tensor_copy(ident_r, ident).then_inc(ident_ready, 1)
        own.mark(v.tensor_scalar(later_b, lcon[:, 1, :], MASKED, None, ALU.mult))
        own.mark(v.tensor_copy(tri_r[:, 0, :], lcon[:, 0, :]))
        own.mark(v.tensor_copy(tri_r[:, 1, :], lcon[:, 0, :]))
        split_t(P_INA, XBC_C)

        dve.wait_ge(dtc_ready, 1)
        v.tensor_copy(dt_c, ps[:, 6, 0:TOK]).then_inc(dtc_evac, 1)
        dve.wait_ge(dt_ready, 1)
        dt_h, dt_l = (ps[:, 7, 0:TOK].rearrange("p (t h) -> p t h", t=NT)[:, :, k * SSM_HEADS:(k + 1) * SSM_HEADS]
                      for k in range(2))
        row = lambda k: dts[:, k, :].rearrange("p (t h) -> p t h", t=NT)
        own.link(v.tensor_tensor(row(0), dt_l, par[:, R_DTB:R_DTB + 24].unsqueeze(1).broadcast_to([P, NT, 24]), ALU.add))
        own.link(v.tensor_tensor(row(0), row(0), dt_h, ALU.add))
        own.link(v.tensor_scalar(dts[:, 9, :], dts[:, 0, :], -1.0, None, ALU.mult))
        v.tensor_tensor(dts[:, 1, :], dts[:, 0, :], dts[:, 9, :], ALU.max).then_inc(dtx_ready, 1)
        own.mark(v.tensor_scalar(dts[:, 11, :], dts[:, 0, :], 0.0, None, ALU.max))
        FIVE = XBC_C // 4
        with dve.Fori(0, 4) as i:
            own.enter(i, 0, FIVE * CONV_W)
            dve.wait_ge(evac_done, i * FIVE + (T_INA + FIVE))
            for k in range(CONV_W):
                own.sync()
                for m in range(FIVE):
                    c = i * FIVE + m
                    src = proj[:, c, k:k + TOK]
                    wk = par[:, bass.ds(c * CONV_W + (C_CONVW + k), 1)]
                    if k == 0:
                        own.mark(v.tensor_scalar(xc[:, c, :], src, wk, par[:, bass.ds(c + C_CONVB, 1)],
                                                 ALU.mult, ALU.add))
                    else:
                        own.mark(v.scalar_tensor_tensor(out=xc[:, c, :], in0=src, scalar=wk, in1=xc[:, c, :],
                                                        op0=ALU.mult, op1=ALU.add))
                for j in (2 * k, 2 * k + 1):
                    lo(i * (2 * BODY) + (P_INA + 2 * XBC_C + j), j % RING)
        own.leave(4)
        own.sync()
        v.tensor_copy(dts[:, 10, 0:1], iota[:, 0:1]).then_inc(conv_done, 1)

        dve.wait_ge(dtl_ready, 1)
        dve.wait_ge(dte_ready, 1)
        own.link(v.tensor_tensor(dts[:, 5, :], dts[:, 11, :], dts[:, 3, :], ALU.add))
        own.link(v.tensor_scalar(dts[:, 4, 24:48], dts[:, 4, 0:24], -1.0, None, ALU.mult))
        v.tensor_tensor(row(6), row(5), dts[:, 4, 24:48].unsqueeze(1).broadcast_to([P, NT, 24]), ALU.mult)\
            .then_inc(adt_ready, 1)
        dve.wait_ge(adth_ready, 1)
        v.tensor_tensor(adt_r[:, 1, :], dts[:, 6, :], adt_r[:, 0, :].bitcast(F32), ALU.subtract).then_inc(adtr_ready, 1)
        for g in range(GROUPS):
            dve.wait_ge(cbo_ready, g + 1)
            v.tensor_tensor(cbm[:, g, :].rearrange("p (a b) -> p a b", a=3)[:, 0:3:2, :],
                            ps[:, 2 + g, 0:384].rearrange("p (a b) -> p a b", a=3)[:, 0:3:2, :],
                            lcon[:, 0, :].unsqueeze(1).broadcast_to([P, 2, P]), ALU.mult).then_inc(cbm_ready, 1)
        dve.wait_ge(cs_ready, 1)
        own.mark(v.tensor_scalar(dts[:, 7, :], ps[:, 6, 0:48], -1.0, None, ALU.mult))
        own.sync()
        v.tensor_copy(dts[:, 8, 0:24], ps[:, 6, 64:88]).then_inc(cs_evac, 1)
        for b in range(6):
            dve.wait_ge(xst_ready, b + 1)
            for t in range(NT):
                ins = v.tensor_tensor(
                    xdt[:, t, 4 * b:4 * b + 4, :].rearrange("p (c h) d -> p c h d", c=2),
                    ps[:, b, :].rearrange("p (c t h d) -> p c t h d", c=2, t=2, h=2)[:, :, t, :, :],
                    dts[:, 5, t * 24 + 4 * b:t * 24 + 4 * b + 4].rearrange("p (c h) -> p c h", c=2)
                    .unsqueeze(3).broadcast_to([P, 2, 2, 64]), ALU.mult)
                if t == 0:
                    own.mark(ins)
                else:
                    own.sync()
                    ins.then_inc(xdt_ready, 1)

        dve.wait_ge(cbo_ready, GROUPS)
        dve.wait_ge(cbm_ready, GROUPS)
        dve.wait_ge(silu_done, 3)

        def gate_y(c):
            dve.wait_ge(y_ready, 2 * c + 2)
            own.link(v.scalar_tensor_tensor(out=cat[:, c, :], in0=xc[:, c, :],
                                            scalar=par[:, C_DSKIP + c:C_DSKIP + c + 1], in1=ps[:, c % 2, 0:TOK],
                                            op0=ALU.mult, op1=ALU.add))
            v.tensor_tensor(cat[:, c, :], cat[:, c, :], proj[:, XBC_C + c, LPAD:LPAD + TOK],
                            ALU.mult).then_inc(y_done, 1)

        for h in range(SSM_HEADS):
            s, c = h % 2, h // 2
            dve.wait_ge(ex_ready, h + 1)
            dve.wait_ge(act_own, 1 + 2 * (h + 1))
            if h >= 2:
                dve.wait_ge(y_ready, h - 1)
            v.tensor_tensor(mt[:, s, :], ex[:, s, :], cbm[:, h // 6, :], ALU.mult).then_inc(m_ready, 1)
            if h % 2 and c >= 1:
                gate_y(c - 1)
        gate_y(MC - 1)
        for g in range(GROUPS):
            dve.wait_ge(rms_ready, g + 1)
            own.link(v.reciprocal(nrm[:, g, :], nrm[:, g, :]))
            for c in range(g * GC, (g + 1) * GC):
                ins = v.scalar_tensor_tensor(out=cat[:, c, :], in0=cat[:, c, :],
                                             scalar=par[:, C_NORMG + c:C_NORMG + c + 1], in1=nrm[:, g, :],
                                             op0=ALU.mult, op1=ALU.mult)
                own.mark(ins)
        attention(0)
        own.sync()
        v.tensor_copy(dts[:, 10, 0:1], iota[:, 0:1]).then_inc(cat_ready, 1)
        dve.wait_ge(o_evac, 2)
        split_n(P_OUT0, 0, S_OUT, lambda i, s: cat[:, i * 2 + s, :])
        norm(0, P_WQ0, P_WQ0)
        split_t(P_WQ0, S_WQ, done=AHEAD)
        experts(0, P_U0, P_V0, S_OUT)
        norm(1, P_INB, P_INB)

        split_t(P_INB, S_INB, done=AHEAD)
        dve.wait_ge(l1_in, 64)
        own.link(v.tensor_copy(ang[:, 2, :], posi))
        own.link(v.tensor_scalar(ang[:, 3, :], ang[:, 2, :], par[:, C_FREQ:C_FREQ + 1], None, ALU.mult))
        for k, (turn, quarter) in enumerate(((0.25, 1.5707963267948966), (0.0, 0.0))):
            own.link(v.tensor_scalar(ang[:, 4, :], ang[:, 3, :], 0.15915494309189535, turn, ALU.mult, ALU.add))
            own.link(v.tensor_scalar(ang[:, 5, :], ang[:, 4, :], 12582912.0, None, ALU.add))
            own.link(v.tensor_scalar(ang[:, 4, :], ang[:, 5, :], -12582912.0, None, ALU.add))
            own.link(v.scalar_tensor_tensor(out=ang[:, 5, :], in0=ang[:, 4, :], scalar=-6.28125, in1=ang[:, 3, :],
                                            op0=ALU.mult, op1=ALU.add))
            own.link(v.scalar_tensor_tensor(out=ang[:, 5, :], in0=ang[:, 4, :], scalar=-0.0019350051879882812,
                                            in1=ang[:, 5, :], op0=ALU.mult, op1=ALU.add))
            own.link(v.scalar_tensor_tensor(out=ang[:, k, :], in0=ang[:, 4, :], scalar=-3.019916050561733e-07,
                                            in1=ang[:, 5, :], op0=ALU.mult, op1=ALU.add))
            own.link(v.tensor_scalar(ang[:, k, :], ang[:, k, :], quarter, 3.1415925, ALU.add, ALU.min))
            ins = v.tensor_scalar(ang[:, k, :], ang[:, k, :], -3.1415925, None, ALU.max)
            if k == 0:
                own.link(ins)
            else:
                ins.then_inc(trig_in, 1)
        dve.wait_ge(cossin_ready, 1)
        dve.wait_ge(evac_done, T_INB + S_INB)
        for n in range(14):
            c = n if n < 2 else n + 2
            own.link(v.tensor_tensor(rtmp[:, n % 2, 0, :], proj1[:, c, :], cs[:, 0, :], ALU.mult))
            dve.wait_ge(rot_ready, n + 1)
            own.link(v.tensor_tensor(rtmp[:, n % 2, 1, :], ps[:, n % 2, 0:TOK], cs[:, 1, :], ALU.mult))
            v.tensor_tensor(proj1[:, c, :], rtmp[:, n % 2, 0, :], rtmp[:, n % 2, 1, :], ALU.add).then_inc(rope_done, 1)
        attention(1)
        dve.wait_ge(o_evac, 16)
        split_n(P_OUT1, S_OUT + S_EXP, S_OUT, lambda i, s: cat[:, i * 2 + s, :])
        norm(2, P_WQ1, P_WQ1)
        split_t(P_WQ1, S_WQ, done=AHEAD)
        experts(1, P_U1, P_V1, 2 * S_OUT + S_EXP)
        norm(3, P_END, None)

    block_cm.__exit__(None, None, None)
    for c in reversed(ctxs):
        c.__exit__(None, None, None)


def shape_constants():
    import numpy as np
    k = np.arange(P)
    ident = np.eye(P)
    iota = np.broadcast_to(k, (P, P))
    tri = k[:, None] <= k[None, :]
    strict = k[:, None] > k[None, :]
    rot = np.zeros((P, P))
    for m in range(P):
        rot[m + 32 if m % 64 < 32 else m - 32, m] = -1.0 if m % 64 < 32 else 1.0
    dup = np.zeros((2, P, P))
    for a in range(2):
        for m in range(P):
            dup[a, a * 64 + m % 64, m] = 1.0
    q = np.arange(TOK) // 64
    seen = (q[None, :] == q[:, None]) | (q[None, :] == q[:, None] - 1)
    mask = np.where(seen, 0.0, MASKED).reshape(NT, P, TOK).transpose(1, 0, 2).reshape(P, 4, P)
    f = np.float32
    base = np.stack([ident, iota], 1).astype(f)
    tris = np.stack([tri, strict], 1).astype(f)
    rcon = np.concatenate([np.stack([rot, dup[0], dup[1]], 1), mask], 1).astype(f)
    inv = (f(1.0) / np.power(f(10000.0), np.arange(0, 64, 2, dtype=f) / f(64))).astype(f)
    return base, tris, rcon, inv[k % 32]


def kernel(x, mem, positions, w_in_a, conv_w, conv_b, dt_bias, a_log, d_skip, ssm_norm_g, w_kv_shared, w_in_b,
           attn_sinks, w_mem_kv, w_out, ln_g, ln_b, peer_wq, peer_subkeys, peer_u, peer_v):
    import numpy as np
    import concourse.bacc as bacc
    from concourse.bass_utils import run_bass_kernel_spmd

    def t_slabs(w):
        n = w.shape[1] // P
        a = np.asarray(w).reshape(2, KC // 2, P, n, P)
        return a.transpose(3, 0, 2, 1, 4).reshape(2 * n, P, PC)

    def n_slabs(w):
        n = w.shape[0] // P
        return np.asarray(w).reshape(n, P, 2, PC).transpose(0, 2, 1, 3).reshape(2 * n, P, PC)

    wa, wb, wkv = np.asarray(w_in_a)[0], np.asarray(w_in_b)[0], np.asarray(w_kv_shared)
    conv_dim = XBC_C * P
    o_c, o_d = MAIN, MAIN + conv_dim
    o_m = o_d + SSM_HEADS
    w = np.concatenate([
        t_slabs(np.asarray(w_mem_kv)[0]), t_slabs(np.asarray(w_mem_kv)[1]),
        t_slabs(wa[:, o_c:o_d]), t_slabs(wa[:, :MAIN]), t_slabs(wa[:, o_m:]),
        n_slabs(w_out[0]), t_slabs(np.asarray(peer_wq)[0]),
        t_slabs(wkv), t_slabs(wb), n_slabs(w_out[1]), t_slabs(np.asarray(peer_wq)[1]),
    ])
    u = np.concatenate([t_slabs(np.asarray(peer_u)[l].T) for l in range(2)])
    vv = np.concatenate([n_slabs(peer_v[l]) for l in range(2)])
    base, tris, rcon, freq = shape_constants()

    def cols(a, c):
        return np.asarray(a).reshape(c, P).T

    par_cols = np.concatenate([
        np.asarray(conv_w)[0].reshape(CONV_W, XBC_C, P).transpose(2, 1, 0).reshape(P, -1),
        cols(conv_b[0], XBC_C),
        cols(np.repeat(np.asarray(d_skip)[0], 64), MC),
        cols(ssm_norm_g[0], MC),
        np.stack([np.asarray(ln_g), np.asarray(ln_b)], 2).reshape(8, KC, P).transpose(2, 0, 1).reshape(P, -1),
        freq[:, None],
    ], 1)
    arrays = {
        "w": w, "u": u, "v": vv,
        "base": base, "tri": tris, "rcon": rcon, "cols": par_cols,
        "rows": np.concatenate([np.asarray(dt_bias)[0], np.asarray(a_log)[0], np.asarray(attn_sinks)[0]]),
        "memT": np.asarray(mem)[0].reshape(TOK, KC, P).transpose(2, 1, 0),
        "xT": np.asarray(x)[0].reshape(TOK, KC, P).transpose(2, 1, 0),
        "dtw": wa[:, o_d:o_m].reshape(KC, P, SSM_HEADS).transpose(1, 0, 2),
        "subk": np.asarray(peer_subkeys).transpose(0, 2, 4, 1, 3).reshape(2, P, PEER_H, KEYS),
        "pos": np.asarray(positions)[0],
    }
    arrays = {f"in_{k}": np.ascontiguousarray(a) for k, a in arrays.items()}
    nc = bacc.Bacc("TRN2", target_bir_lowering=False, num_devices=1, dynamic_dma_scratch_size=64)
    dram = {}
    for k, a in arrays.items():
        dram[k[3:]] = nc.dram_tensor(k, a.shape, mybir.dt.from_np(a.dtype), kind="ExternalInput").ap()
    dram["out"] = nc.dram_tensor("out_x", (P, KC, TOK), F32, kind="ExternalOutput").ap()
    dram["h"] = nc.dram_tensor("h_scratch", (S_EXP, P, TOK), F32, kind="Internal").ap()
    dram["spill"] = nc.dram_tensor("kv_scratch", (P, 2048), F32, kind="Internal").ap()
    build(nc, dram)
    r = run_bass_kernel_spmd(nc, [arrays], core_ids=[0])
    got = r.results[0]["out_x"]
    return np.ascontiguousarray(got.transpose(2, 1, 0).reshape(1, TOK, D))
```
